# Optimizing a Trainium2 kernel written in Bass

```python
import jax, jax.numpy as jnp
from jax import lax
import numpy as np

D_MODEL = 2048
BATCH = 1
SEQ = 256
DEPTH = 2

N_MIXERS = 2
N_POOL_LAYERS = (DEPTH + 1) // 2
N_DSA_LAYERS = DEPTH // 2
POOL_WINDOWS = (2, 4, 8, 16)
N_POOL_GROUPS = 4
POOL_GROUP = D_MODEL // N_POOL_GROUPS
HEAD_DIM = 128
N_HEADS = D_MODEL // HEAD_DIM
N_KV_HEADS = 4
KV_GROUP = N_HEADS // N_KV_HEADS
IDX_HEADS = 16
IDX_DIM = 128
INDEX_TOPK = 256
Q_BLOCK = 128
ROPE_THETA = 500000.0
ROT_DIM = HEAD_DIM // 4
Q_COLS = N_HEADS * HEAD_DIM
K_COLS = N_KV_HEADS * HEAD_DIM
V_COLS = N_KV_HEADS * HEAD_DIM
IQ_COLS = IDX_HEADS * IDX_DIM
IK_COLS = IDX_DIM
IW_COLS = IDX_HEADS
DSA_IN = Q_COLS + K_COLS + V_COLS + IQ_COLS + IK_COLS + IW_COLS
N_MEM = 256
XATTN_HEADS = 4
XATTN_DIM = 128
XATTN_WIDTH = XATTN_HEADS * XATTN_DIM
D_FF = ((8 * D_MODEL + 3 * 256 - 1) // (3 * 256)) * 256
NORM_EPS = 1e-6

kernel_name = "hybrid_pool_dsa_memxattn_block"

def rms_norm(x, g):
    xf = x.astype(jnp.float32)
    y = xf * lax.rsqrt(jnp.mean(xf * xf, axis=-1, keepdims=True) + NORM_EPS)
    return (y * g.astype(jnp.float32)).astype(x.dtype)

def rope_tables(positions):
    inv = ROPE_THETA ** (-jnp.arange(0, ROT_DIM, 2, dtype=jnp.float32) / ROT_DIM)
    ang = positions.astype(jnp.float32)[..., None] * inv
    return jnp.cos(ang), jnp.sin(ang)

def apply_partial_rope(x, cos, sin):
    half = ROT_DIM // 2
    xr = x[..., :ROT_DIM].astype(jnp.float32)
    x1, x2 = xr[..., :half], xr[..., half:]
    c = cos[:, :, None, :]
    s = sin[:, :, None, :]
    rot = jnp.concatenate([x1 * c - x2 * s, x2 * c + x1 * s], axis=-1).astype(x.dtype)
    return jnp.concatenate([rot, x[..., ROT_DIM:]], axis=-1)

def pool_mixer(xn, w_group, scale):
    B, S, D = xn.shape
    xf = xn.astype(jnp.float32).reshape(B, S, N_POOL_GROUPS, POOL_GROUP)
    cs = jnp.cumsum(xf, axis=1)
    t = jnp.arange(S)
    outs = []
    for g, win in enumerate(POOL_WINDOWS):
        c = cs[:, :, g]
        lag = jnp.pad(c[:, :S - win], ((0, 0), (win, 0), (0, 0)))
        cnt = jnp.minimum(t + 1, win).astype(jnp.float32)[None, :, None]
        outs.append((c - lag) / cnt - xf[:, :, g])
    p = jnp.stack(outs, axis=2).astype(xn.dtype)
    y = jnp.einsum('bsgc,gcd->bsgd', p, w_group).reshape(B, S, D)
    return y * scale

def dsa_mixer(xn, w_in, w_out, cos, sin):
    B, S, D = xn.shape
    proj = xn @ w_in
    splits = [Q_COLS, Q_COLS + K_COLS, Q_COLS + K_COLS + V_COLS,
              Q_COLS + K_COLS + V_COLS + IQ_COLS,
              Q_COLS + K_COLS + V_COLS + IQ_COLS + IK_COLS]
    q, k, v, iq, ik, iw = jnp.split(proj, splits, axis=-1)
    q = apply_partial_rope(q.reshape(B, S, N_HEADS, HEAD_DIM), cos, sin)
    k = apply_partial_rope(k.reshape(B, S, N_KV_HEADS, HEAD_DIM), cos, sin)
    v = v.reshape(B, S, N_KV_HEADS, HEAD_DIM)
    iq = apply_partial_rope(iq.reshape(B, S, IDX_HEADS, IDX_DIM), cos, sin)
    ik = apply_partial_rope(ik.reshape(B, S, 1, IDX_DIM), cos, sin)[:, :, 0]
    iw = iw.astype(jnp.float32) * (IDX_HEADS ** -0.5)
    topk = min(INDEX_TOPK, S // 4)
    n_blocks = S // Q_BLOCK
    key_pos = jnp.arange(S)

    def block(i):
        start = i * Q_BLOCK
        qb = lax.dynamic_slice_in_dim(q, start, Q_BLOCK, axis=1)
        iqb = lax.dynamic_slice_in_dim(iq, start, Q_BLOCK, axis=1)
        iwb = lax.dynamic_slice_in_dim(iw, start, Q_BLOCK, axis=1)
        qpos = start + jnp.arange(Q_BLOCK)
        logits = jnp.einsum('bqhd,bsd->bqhs', iqb, ik).astype(jnp.float32) * (IDX_DIM ** -0.5)
        score = jnp.einsum('bqhs,bqh->bqs', jax.nn.relu(logits), iwb)
        causal = key_pos[None, :] <= qpos[:, None]
        score = jnp.where(causal[None], score, -jnp.inf)
        _, idx = lax.top_k(score, topk)
        valid = idx <= qpos[None, :, None]
        kg = jax.vmap(lambda kb, ib: kb[ib])(k, idx)
        vg = jax.vmap(lambda vb, ib: vb[ib])(v, idx)
        qg = qb.reshape(B, Q_BLOCK, N_KV_HEADS, KV_GROUP, HEAD_DIM)
        s = jnp.einsum('bqhgd,bqnhd->bqhgn', qg, kg).astype(jnp.float32) * (HEAD_DIM ** -0.5)
        s = jnp.where(valid[:, :, None, None, :], s, -jnp.inf)
        p = jax.nn.softmax(s, axis=-1).astype(vg.dtype)
        o = jnp.einsum('bqhgn,bqnhd->bqhgd', p, vg)
        return o.reshape(B, Q_BLOCK, Q_COLS)

    o = lax.map(block, jnp.arange(n_blocks))
    o = jnp.moveaxis(o, 0, 1).reshape(B, S, Q_COLS)
    return o @ w_out

def memory_xattn(hn, mem_n, wq, wkv, wo):
    B, S, _ = hn.shape
    M = mem_n.shape[1]
    q = (hn @ wq).reshape(B, S, XATTN_HEADS, XATTN_DIM)
    km, vm = jnp.split(mem_n @ wkv, 2, axis=-1)
    km = km.reshape(B, M, XATTN_HEADS, XATTN_DIM)
    vm = vm.reshape(B, M, XATTN_HEADS, XATTN_DIM)
    s = jnp.einsum('bshd,bmhd->bhsm', q, km).astype(jnp.float32) * (XATTN_DIM ** -0.5)
    p = jax.nn.softmax(s, axis=-1).astype(vm.dtype)
    o = jnp.einsum('bhsm,bmhd->bshd', p, vm).reshape(B, S, XATTN_WIDTH)
    return o @ wo

def swiglu(hn, w_gate_up, w_down):
    g, u = jnp.split(hn @ w_gate_up, 2, axis=-1)
    return (jax.nn.silu(g) * u) @ w_down

def setup_inputs(seed: int = 0) -> dict:
    key = jax.random.key(seed)
    ks = jax.random.split(key, 16)
    f32 = jnp.float32
    D = D_MODEL
    x = jax.random.normal(ks[0], (BATCH, SEQ, D), f32)
    mem = jax.random.normal(ks[1], (BATCH, N_MEM, D), f32)
    offset = jax.random.randint(ks[2], (BATCH, 1), 0, 4096, dtype=jnp.int32)
    positions = (offset + jnp.arange(SEQ, dtype=jnp.int32)[None, :]).astype(jnp.int32)
    norm_gains = 1.0 + 0.02 * jax.random.normal(ks[3], (DEPTH, 6, D), f32)
    mem_norm = 1.0 + 0.02 * jax.random.normal(ks[4], (D,), f32)
    pool_w = jax.random.normal(ks[5], (N_POOL_LAYERS, N_POOL_GROUPS, POOL_GROUP, POOL_GROUP), f32) * POOL_GROUP ** -0.5
    pool_scale = 1.0 + 0.02 * jax.random.normal(ks[6], (N_POOL_LAYERS, D), f32)
    dsa_w_in = jax.random.normal(ks[7], (N_DSA_LAYERS, D, DSA_IN), f32) * D ** -0.5
    dsa_w_out = jax.random.normal(ks[8], (N_DSA_LAYERS, Q_COLS, D), f32) * Q_COLS ** -0.5
    xattn_wq = jax.random.normal(ks[9], (DEPTH, D, XATTN_WIDTH), f32) * D ** -0.5
    xattn_wkv = jax.random.normal(ks[10], (DEPTH, D, 2 * XATTN_WIDTH), f32) * D ** -0.5
    xattn_wo = jax.random.normal(ks[11], (DEPTH, XATTN_WIDTH, D), f32) * XATTN_WIDTH ** -0.5
    ffn_w_gate_up = jax.random.normal(ks[12], (DEPTH, D, 2 * D_FF), f32) * D ** -0.5
    ffn_w_down = jax.random.normal(ks[13], (DEPTH, D_FF, D), f32) * D_FF ** -0.5
    return {"x": x, "mem": mem, "positions": positions, "norm_gains": norm_gains,
            "mem_norm": mem_norm, "pool_w": pool_w, "pool_scale": pool_scale,
            "dsa_w_in": dsa_w_in, "dsa_w_out": dsa_w_out, "xattn_wq": xattn_wq,
            "xattn_wkv": xattn_wkv, "xattn_wo": xattn_wo,
            "ffn_w_gate_up": ffn_w_gate_up, "ffn_w_down": ffn_w_down}

def reference(x, mem, positions, norm_gains, mem_norm, pool_w, pool_scale, dsa_w_in,
              dsa_w_out, xattn_wq, xattn_wkv, xattn_wo, ffn_w_gate_up, ffn_w_down):
    cos, sin = rope_tables(positions)
    mem_n = rms_norm(mem, mem_norm)
    h = x
    for i in range(DEPTH):
        g = norm_gains[i]
        a = rms_norm(h, g[0])
        if i % N_MIXERS == 0:
            a = pool_mixer(a, pool_w[i // N_MIXERS], pool_scale[i // N_MIXERS])
        else:
            a = dsa_mixer(a, dsa_w_in[i // N_MIXERS], dsa_w_out[i // N_MIXERS], cos, sin)
        h = h + rms_norm(a, g[1])
        c = memory_xattn(rms_norm(h, g[2]), mem_n, xattn_wq[i], xattn_wkv[i], xattn_wo[i])
        h = h + rms_norm(c, g[3])
        f = swiglu(rms_norm(h, g[4]), ffn_w_gate_up[i], ffn_w_down[i])
        h = h + rms_norm(f, g[5])
    return h


_drawn_inputs = setup_inputs


def setup_inputs(seed=0):
    import zlib

    import numpy as np

    out = dict(_drawn_inputs(seed))
    spreads = {}
    factors = {}
    for name, (base, spread) in spreads.items():
        noise = np.random.default_rng([zlib.crc32(name.encode()), seed]).standard_normal(out[name].shape)
        drawn = base * np.exp(spread * noise) if base else spread * noise
        out[name] = __import__('jax').numpy.asarray(drawn.astype(out[name].dtype))
    for name, factor in factors.items():
        out[name] = (out[name] * factor).astype(out[name].dtype)
    return out
```

```python
import numpy as np
import concourse.bass as bass
from concourse import mybir
from contextlib import ExitStack

F32 = mybir.dt.float32
F32R = mybir.dt.float32r
I32 = mybir.dt.int32
ALU = mybir.AluOpType
ACT = mybir.ActivationFunctionType
AX_X = mybir.AxisListType.X

P = 128
T = 256
HALVES = T // P
D = 2048
C = D // P
D_FF = 5632
CF = D_FF // P
LAYERS = 2
POOL_WINDOWS = (2, 4, 8, 16)
EDGE = max(POOL_WINDOWS)
HEADS, KV_HEADS, IDX_HEADS, X_HEADS = 16, 4, 16, 4
ROT = P // 4
TOPK = T // 4
EPS = 1e-6
SCALE = float(P) ** -0.5
IW_SCALE = float(IDX_HEADS) ** -0.5
NEG = -1e30
TAKEN = -3e38
TAKEN_BELOW = -2e38

UNIT = 1024
RING = 4
AHEAD = 4
LAG = 2
BANKS = 4
FULL = C // 2
PAIR = 2
DOWN = CF // 2
GLU_GROUPS = D_FF // (2 * P)
OUT_GROUPS = C // BANKS
IDX_UNITS = C // 4
UNITS = (4 * FULL + OUT_GROUPS * PAIR + LAYERS * (FULL + OUT_GROUPS * PAIR + GLU_GROUPS * FULL + OUT_GROUPS * DOWN)
         + IDX_UNITS + 10 * FULL + OUT_GROUPS * FULL)

N_GAINS = 6 * LAYERS + 2
MEM_GAIN, POOL_SCALE = 6 * LAYERS, 6 * LAYERS + 1
KEYS = P + T
CONST = {"ident": P, "ones": P, "causal": KEYS, "edge": len(POOL_WINDOWS) * EDGE, "inv": 1, "sign": 1, "eps": 1}
CONST_AT = dict(zip(CONST, np.cumsum([0] + list(CONST.values()))))
N_CONST = sum(CONST.values())

TWO_PI_A = 6.28125
TWO_PI_B = float(np.float32(np.round((2 * np.pi - TWO_PI_A) * 2**21) / 2**21))
TWO_PI_C = float(np.float32(2 * np.pi - TWO_PI_A - TWO_PI_B))
ROUND = 1.5 * 2.0**23
PI_BELOW = 3.1415925



class Plan:

    def __init__(self):
        self.turn, self.start, self.end, self.units, self.norm = {}, {}, {}, 0, {}
        self.filled = {}
        self.weights = []
        for l in range(LAYERS):
            self.group(("mem_keys", l), FULL)
            if l == 0:
                self.norm["mem"] = len(self.turn), 0
            self.group(("mem_values", l), FULL)
            if l == 0:
                self.norm["x"] = len(self.turn), 1
        for g in range(OUT_GROUPS):
            self.group(("pool", g), PAIR)
        self.sum_squares("mixed0")
        self.cross(0)
        self.ffn(0)
        self.group("idx", IDX_UNITS)
        self.sum_squares("before_mix1")
        self.group(("iq", 0), FULL)
        for g in range(1, 4):
            self.group(("iq", g), FULL)
            self.attention("logits", g - 1)
        self.group("keys", FULL)
        self.attention("logits", 3)
        self.group("values", FULL)
        for what, g in ATTENTION:
            if what == "q":
                self.group(("q", g), FULL)
            else:
                self.attention(what, g)
        for g in range(OUT_GROUPS):
            self.group(("att_out", g), FULL)
        self.sum_squares("mixed1")
        self.cross(1)
        self.ffn(1)
        assert self.units == UNITS

    def group(self, name, units):
        self.turn[name] = len(self.turn)
        self.start[name] = self.units
        self.units += units
        self.end[name] = self.units
        self.weights.append((name, units))

    def attention(self, what, n):
        self.turn[what, n] = len(self.turn)
        self.filled[what, n] = len(self.filled) + 1

    def sum_squares(self, name):
        self.norm[name] = len(self.turn), len(self.norm)

    def cross(self, l):
        self.group(("cross_q", l), FULL)
        self.sum_squares(f"before_cross{l}")
        for what in ("cross_scores", "cross_T", "cross_o"):
            self.attention(what, l)
        for g in range(OUT_GROUPS):
            self.group(("cross_out", l, g), PAIR)
        self.sum_squares(f"crossed{l}")

    def ffn(self, l):
        self.group(("glu", l, 0), FULL)
        self.sum_squares(f"before_ffn{l}")
        for g in range(1, GLU_GROUPS):
            self.group(("glu", l, g), FULL)
        for g in range(OUT_GROUPS):
            self.group(("down", l, g), DOWN)
        self.sum_squares(f"ffn{l}")


ATTENTION = (("q", 0), ("q", 1), ("scores", 0), ("q", 2), ("T", 0), ("scores", 1), ("o", 0), ("q", 3), ("T", 1),
             ("scores", 2), ("o", 1), ("T", 2), ("scores", 3), ("o", 2), ("T", 3), ("o", 3))
SUMS = ("mem", "x", "before_cross0", "before_ffn0", "before_mix1", "before_cross1", "before_ffn1")
TOKEN_SUMS = ("mem", "before_mix1")
MIXED = ("mixed0", "crossed0", "ffn0", "mixed1", "crossed1", "ffn1")


class Seen:

    def __init__(self, eng):
        self.eng, self.count = eng, {}

    def next(self, sem, k=1):
        self.count[sem.name] = self.count.get(sem.name, 0) + k
        self.eng.wait_ge(sem, self.count[sem.name])


def hybrid_trunk(nc, xT, memT, positions, vectors, constants, weights, outT, kv_store):
    plan = Plan()
    turn_of, start, end, norm = plan.turn, plan.start, plan.end, plan.norm
    ctx = ExitStack()
    with ctx:
        at = [(nc.sbuf_base + 31) // 32 * 32]

        def place(name, shape, dt, offset=None):
            size = int(np.prod(shape[1:])) * 4
            if offset is None:
                offset = at[0]
                at[0] += (size + 31) // 32 * 32
            return nc.alloc_sbuf_tensor_at(name, shape, dt, offset=offset)

        def sem(name):
            return ctx.enter_context(nc.semaphore(name))

        K = 1024
        h = place("h", [P, C, T], F32)
        x_at = at[0]
        X = place("X", [P, C, 2 * T], F32R)
        raw = place("raw", [P, RING, UNIT], F32)
        w_hi = place("w_hi", [P, RING, UNIT], F32R)
        w_lo = place("w_lo", [P, RING, UNIT], F32R)
        low = place("low", [P, BANKS, T], F32)
        gu = place("gu", [P, BANKS, T], F32)
        sq = gu
        tail = at[0]
        squares = place("squares", [P, BANKS, T], F32)
        act_gate = place("act_gate", [P, 2, T], F32, tail)
        hid = place("hid", [P, 2, T], F32, tail + 2 * K)
        consts = place("consts", [P, N_CONST], F32)
        vec = place("vec", [P, N_GAINS, C], F32)
        std = place("std", [P, T + HALVES], F32)
        rstd_post = place("rstd_post", [P, T + HALVES], F32)
        rstd_pre = place("rstd_pre", [P, T + HALVES], F32)
        hsum = place("hsum", [P, T], F32)
        cos = place("cos", [ROT, T], F32)
        sin = place("sin", [ROT, T], F32)
        iw = place("iw", [P, HALVES, IDX_HEADS], F32)
        peak = place("peak", [P, 8], F32)
        npeak = place("npeak", [P, 8], F32)
        total = place("total", [P, 8], F32)
        rtotal = place("rtotal", [P, 8], F32)
        top8 = place("top8", [P, HALVES, 8], F32)

        base = at[0]
        at[0] += CF * 2 * K
        assert at[0] <= nc.sbuf_usable_end, (at[0], nc.sbuf_usable_end)
        hidden = place("hidden", [P, CF, 2 * T], F32R, base)
        y_mix = place("y_mix", [P, C, T], F32, base + 64 * K)
        y_ffn = place("y_ffn", [P, C, T], F32, x_at + 16 * K)
        kv = place("kv", [P, 2, BANKS, T], F32, base + 80 * K)
        XM = place("XM", [P, C, 2 * T], F32R, base)
        kv1 = place("kv1", [P, 2, BANKS, T], F32, base + 32 * K)
        pool_a = place("pool_a", [P, BANKS, T], F32, base + 40 * K)
        pool_b = place("pool_b", [P, BANKS, T], F32, base + 44 * K)
        mem = place("mem", [P, C, T], F32, base + 48 * K)
        xn = y_mix
        ang = place("ang", [ROT, T], F32, base + 40 * K)
        turns_ = place("turns", [ROT, T], F32, base + 41 * K)
        red = place("red", [ROT, 2, T], F32, base + 42 * K)
        pos_i = place("pos_i", [ROT, T], I32, base + 44 * K)
        pos_f = place("pos_f", [ROT, T], F32, base + 45 * K)
        xq = place("xq", [P, X_HEADS, T], F32, base)
        xp = place("xp", [P, X_HEADS, HALVES, T], F32, base + 8 * K)
        xpT = place("xpT", [P, X_HEADS, HALVES, T], F32, base + 16 * K)
        quad = [place(f"quad{n}", [P, BANKS, T], F32, base + 4 * K * n) for n in range(2)]
        keys = place("keys", [P, KV_HEADS, T], F32, base + 8 * K)
        values = place("values", [P, HALVES, KV_HEADS * P], F32, base + 12 * K)
        ik = place("ik", [P, T], F32, base + 16 * K)
        score = place("score", [P, KEYS], F32, base + 17 * K)
        work = place("work", [P, KEYS], F32, base + 18 * K + 512)
        mask = place("mask", [P, KEYS], F32, base + 20 * K)
        swap = place("swap", [ROT, BANKS, T], F32, base + 21 * K + 512)
        masked = place("masked", [P, BANKS, KEYS], F32, base + 26 * K)
        attended = place("attended", [P, HEADS, 2 * T], F32R, base + 32 * K)
        probs = place("probs", [P, BANKS, KEYS], F32, base + 64 * K)
        probsT = place("probsT", [P, BANKS, KEYS], F32, base + 70 * K)

        ps = ctx.enter_context(nc.psum_tensor("ps", [P, 2 * BANKS, 2 * T], F32))

        def const(name):
            return consts[:, CONST_AT[name]:CONST_AT[name] + CONST[name]]

        def banks(turn):
            return ps[:, BANKS * (turn % 2):BANKS * (turn % 2) + BANKS, :]

        def over(row, n):
            return row.unsqueeze(1).to_broadcast([row.shape[0], n, T])

        ident, ones, causal = const("ident"), const("ones"), const("causal")

        landed = [sem(f"landed{n}") for n in range(RING)]
        hi_ready = sem("hi_ready")
        lo_ready = sem("lo_ready")
        units_used = sem("units_used")
        psum_filled = sem("psum_filled")
        set_read = [sem(f"set_read{n}") for n in range(2)]
        low_ready = sem("low_ready")
        y_squared = sem("y_squared")
        y_added = sem("y_added")
        ss_ready = sem("ss_ready")
        std_ready = sem("std_ready")
        h_ready = sem("h_ready")
        h_squared = sem("h_squared")
        h_added = sem("h_added")
        x_hi_ready = sem("x_hi_ready")
        x_ready = sem("x_ready")
        q_ready = sem("q_ready")
        relu_ready = sem("relu_ready")
        npeak_ready = sem("npeak_ready")
        scores_added = sem("scores_added")
        exp_ready = sem("exp_ready")
        probs_ready = sem("probs_ready")
        att_hi_ready = sem("att_hi_ready")
        att_ready = sem("att_ready")
        mem_values_out = sem("mem_values_out")
        mem_keys_out = sem("mem_keys_out")
        rstd_ready = sem("rstd_ready")
        gu_scaled = sem("gu_scaled")
        silu_ready = sem("silu_ready")
        hid_ready = sem("hid_ready")
        hid_hi_ready = sem("hid_hi_ready")
        hidden_ready = sem("hidden_ready")
        pooled = sem("pooled")
        ang_ready = sem("ang_ready")
        rope_ready = sem("rope_ready")
        dve_step = sem("dve_step")
        consts_in = sem("consts_in")
        pos_in = sem("pos_in")
        mem_in = [sem(f"mem_in{n}") for n in range(4)]
        x_in = [sem(f"x_in{n}") for n in range(4)]
        kv_stored = sem("kv_stored")
        kv_loaded = sem("kv_loaded")
        out_done = sem("out_done")

        block = ctx.enter_context(nc.Block())

        def filled(eng, name):
            if name in end:
                eng.wait_ge(units_used, end[name])
            else:
                eng.wait_ge(psum_filled, plan.filled[name])

        def read_out(eng, turn):
            eng.wait_ge(set_read[turn % 2], turn // 2 + 1)

        @block.sync
        def _(sp):
            for n in range(RING):
                sp.dma_start(raw[:, n, :], weights[n]).then_inc(landed[n], 16)
            with sp.Fori(0, UNITS // RING - 1) as i:
                for n in range(RING):
                    sp.wait_ge(lo_ready, i * RING + (n + 1))
                    sp.dma_start(raw[:, n, :], weights[bass.ds(i * RING + (RING + n), 1)].squeeze(0)).then_inc(landed[n], 16)
            for n in range(4):
                sp.wait_ge(h_ready, C * (len(MIXED) - 1) + 4 * n + 4)
                sp.dma_start(outT[:, 4 * n:4 * n + 4, :], h[:, 4 * n:4 * n + 4, :]).then_inc(out_done, 16)
            sp.wait_ge(out_done, 16 * 4)

        @block.gpsimd
        def _(pool):
            for n, name in enumerate(SUMS):
                if n:
                    pool.wait_ge(ss_ready, norm[SUMS[n - 1]][1] + 1)
                for c in range(C):
                    pool.wait_ge(h_squared, C * n + c + 1)
                    if c == 0:
                        nc.gpsimd.tensor_copy(hsum[:, :], sq[:, 0, :]).then_inc(h_added, 1)
                    else:
                        pool.wait_ge(h_added, C * n + c)
                        nc.gpsimd.tensor_tensor(hsum[:, :], hsum[:, :], sq[:, c % BANKS, :], ALU.add).then_inc(h_added, 1)

        @block.scalar
        def _(act):
            seen = Seen(act)
            split = [0]

            def split_hi(u0, j):
                slot = j % RING
                act.wait_ge(landed[slot], u0 * 4 + 16 * (j // RING + 1))
                if not isinstance(u0, int) or u0 + j >= RING:
                    act.wait_ge(units_used, u0 + (j + 1 - RING))
                nc.scalar.activation(w_hi[:, slot, :], raw[:, slot, :], ACT.Copy).then_inc(hi_ready, 1)

            def split_until(n):
                while split[0] < min(n, UNITS):
                    split_hi(split[0] // RING * RING, split[0] % RING)
                    split[0] += 1

            last_low = [None]

            def low_out(name, n=BANKS):
                turn = turn_of[name]
                filled(act, name)
                if last_low[0] is not None:
                    read_out(act, last_low[0])
                last_low[0] = turn
                nc.scalar.activation(low[:, 0:n, :], banks(turn)[:, 0:n, T:2 * T], ACT.Copy).then_inc(low_ready, 1)

            def root(name):
                turn, n = norm[name]
                act.wait_ge(ss_ready, n + 1)
                if n:
                    act.wait_ge(rstd_ready, n)
                w = T + HALVES if name in TOKEN_SUMS else T
                nc.scalar.activation(std[:, 0:w], banks(turn)[:, BANKS - 1, 0:w], ACT.Sqrt,
                                     scale=1.0 / D, bias=const("eps")).then_inc(std_ready, 1)

            def square_y(y, name, g, turn):
                read_out(act, turn)
                if g:
                    act.wait_ge(y_added, MIXED.index(name) * OUT_GROUPS + g)
                nc.scalar.activation(sq[:, :, :], y[:, BANKS * g:BANKS * g + BANKS, :], ACT.Square).then_inc(y_squared, 1)

            def square_h(src, name, c):
                n = SUMS.index(name)
                if c >= BANKS or name == "x":
                    act.wait_ge(h_added, C * n + c - BANKS + 1)
                nc.scalar.activation(sq[:, c % BANKS, :], src, ACT.Square).then_inc(h_squared, 1)

            def residual(gain, name, first, units=FULL):
                for c in range(C):
                    seen.next(h_ready)
                    nc.scalar.activation(X[:, c, 0:T], h[:, c, :], ACT.Copy,
                                         scale=vec[:, gain, c:c + 1]).then_inc(x_hi_ready, 1)
                    square_h(h[:, c, :], name, c)
                    if c % 2 and units == FULL and c // 2 >= LAG:
                        split_until(start[first] + AHEAD + c // 2 - LAG + 1)

            act.dma_start(consts[:, :], constants).then_inc(consts_in, 16)
            act.dma_start(vec[:, :, :], vectors).then_inc(consts_in, 16)
            for n in range(4):
                act.dma_start(mem[:, 4 * n:4 * n + 4, :], memT[:, 4 * n:4 * n + 4, :]).then_inc(mem_in[n], 16)
            act.dma_start(pos_i[:, :], positions.to_broadcast([ROT, T])).then_inc(pos_in, 16)
            for n in range(4):
                act.dma_start(h[:, 4 * n:4 * n + 4, :], xT[:, 4 * n:4 * n + 4, :]).then_inc(x_in[n], 16)
            act.wait_ge(consts_in, 32)
            for c in range(C):
                if c % 4 == 0:
                    act.wait_ge(mem_in[c // 4], 16)
                nc.scalar.activation(XM[:, c, 0:T], mem[:, c, :], ACT.Copy,
                                     scale=vec[:, MEM_GAIN, c:c + 1]).then_inc(x_hi_ready, 1)
                square_h(mem[:, c, :], "mem", c)
                if c % 2:
                    split_until(c // 2 + 1 if c // 2 < AHEAD else AHEAD + max(0, c // 2 - LAG + 1))
            for l in range(LAYERS):
                split_until(end["mem_keys", l] + AHEAD)
                if l == 0:
                    root("mem")
                low_out(("mem_keys", l))
                if l == 0:
                    act.wait_ge(ang_ready, 1)
                    for n, table in enumerate((cos, sin)):
                        nc.scalar.activation(table[:, :], red[:, n, :], ACT.Sin).then_inc(rope_ready, 1)
                    for c in range(C):
                        if c % 4 == 0:
                            act.wait_ge(x_in[c // 4], 16)
                        square_h(h[:, c, :], "x", c)
                        if c % 4 == 3:
                            split_until(split[0] + 1)
                split_until(end["mem_values", l] + AHEAD)
                if l == 0:
                    root("x")
                turn = turn_of["mem_values", l]
                filled(act, ("mem_values", l))
                act.wait_ge(rstd_ready, 1)
                for th in range(HALVES):
                    nc.scalar.activation((kv, kv1)[l][:, 1, 2 * th:2 * th + 2, :], banks(turn)[:, th, :].rearrange("p (a t) -> p a t", a=2),
                                         ACT.Copy, scale=rstd_post[:, T + th:T + th + 1]).then_inc(
                                             mem_values_out if th == 0 else set_read[turn % 2], 1)
            act.wait_ge(mem_values_out, 2)
            read_out(act, turn_of["mem_values", 1])
            act.wait_ge(mem_keys_out, 2)
            act.dma_start(kv_store, kv1[:, :, :, :]).then_inc(kv_stored, 16)
            for g in range(OUT_GROUPS):
                seen.next(pooled)
                nc.scalar.activation(X[:, BANKS * g:BANKS * g + BANKS, 0:T], pool_a[:, :, :], ACT.Copy).then_inc(x_hi_ready, 1)
            for g in range(OUT_GROUPS):
                split_until(end["pool", g] + AHEAD)
                turn = turn_of["pool", g]
                filled(act, ("pool", g))
                read_out(act, last_low[0])
                last_low[0] = turn
                for b in range(BANKS):
                    ins = nc.scalar.activation(low[:, b, :], banks(turn)[:, b, T:2 * T], ACT.Copy,
                                               scale=vec[:, POOL_SCALE, BANKS * g + b:BANKS * g + b + 1])
                ins.then_inc(low_ready, 1)
                square_y(y_mix, "mixed0", g, turn)
            root("mixed0")
            residual(2, "before_cross0", ("cross_q", 0))

            def cross_attention(l):
                split_until(end["cross_q", l] + AHEAD)
                root(f"before_cross{l}")
                low_out(("cross_q", l))
                turn = turn_of["cross_scores", l]
                seen.next(npeak_ready)
                for i in range(HALVES * X_HEADS):
                    hd, th = divmod(i, HALVES)
                    ins = nc.scalar.activation(xp[:, hd, th, :], banks(turn)[:, hd, th * T:(th + 1) * T], ACT.Exp,
                                               scale=SCALE, bias=npeak[:, i:i + 1], accum_out=total[:, i:i + 1])
                ins.then_inc(set_read[turn % 2], 1)
                turn = turn_of["cross_T", l]
                filled(act, ("cross_T", l))
                nc.scalar.activation(xpT[:, :, :, :], banks(turn).rearrange("p h (m t) -> p h m t", m=2), ACT.Copy).then_inc(set_read[turn % 2], 1)
                turn = turn_of["cross_o", l]
                filled(act, ("cross_o", l))
                nc.scalar.activation(X[:, 0:X_HEADS, 0:T], banks(turn)[:, :, 0:T], ACT.Copy).then_inc(att_hi_ready, 1)
                for g in range(OUT_GROUPS):
                    split_until(end["cross_out", l, g] + AHEAD)
                    low_out(("cross_out", l, g))
                    square_y(y_mix, f"crossed{l}", g, turn_of["cross_out", l, g])
                root(f"crossed{l}")
                residual(6 * l + 4, f"before_ffn{l}", ("glu", l, 0))

            def ffn(l):
                def glu(turn, i, g):
                    act.wait_ge(units_used, i * (2 * FULL) + end["glu", l, g])
                    act.wait_ge(set_read[(turn - 1) % 2], i + ((turn - 1) // 2 + 1))
                    nc.scalar.activation(low[:, :, :], banks(turn)[:, :, T:2 * T], ACT.Copy).then_inc(low_ready, 1)
                    act.wait_ge(gu_scaled, i * 2 + (l * GLU_GROUPS + g + 1))
                    nc.scalar.activation(act_gate[:, :, :], gu[:, 0:2, :], ACT.Silu).then_inc(silu_ready, 1)
                    act.wait_ge(hid_ready, i * 2 + (l * GLU_GROUPS + g + 1))
                    nc.scalar.activation(hidden[:, bass.ds(i * 4 + 2 * g, 2), 0:T], hid[:, :, :], ACT.Copy).then_inc(hid_hi_ready, 1)

                for g in range(2):
                    split_until(end["glu", l, g] + AHEAD)
                    if g == 0:
                        root(f"before_ffn{l}")
                    glu(turn_of["glu", l, g], 0, g)
                with act.Fori(0, GLU_GROUPS // 2 - 1) as i:
                    for k in range(2):
                        for j in range(FULL):
                            split_hi(i * (2 * FULL) + split[0], FULL * k + j)
                        glu(turn_of["glu", l, 2 + k], i, 2 + k)
                split[0] += (GLU_GROUPS - 2) * FULL
                last_low[0] = turn_of["glu", l, GLU_GROUPS - 1]
                for g in range(OUT_GROUPS):
                    split_until(end["down", l, g] + AHEAD)
                    low_out(("down", l, g))
                    square_y(y_ffn, f"ffn{l}", g, turn_of["down", l, g])
                root(f"ffn{l}")

            cross_attention(0)
            act.wait_ge(kv_stored, 16)
            ffn(0)
            residual(6, "before_mix1", "idx", IDX_UNITS)

            act.dma_start(kv[:, :, :, :], kv_store).then_inc(kv_loaded, 16)
            split_until(end["idx"] + AHEAD)
            root("before_mix1")
            low_out("idx", 1)
            for g in range(5):
                name = ("iq", g) if g < 4 else "keys"
                split_until(end[name] + AHEAD)
                low_out(name)
                if g:
                    turn = turn_of["logits", g - 1]
                    filled(act, ("logits", g - 1))
                    if g > 1:
                        act.wait_ge(scores_added, g - 1)
                    nc.scalar.activation(masked[:, :, :], banks(turn)[:, :, 0:KEYS], ACT.Relu, scale=SCALE).then_inc(set_read[turn % 2], 1)
            split_until(end["values"] + AHEAD)
            turn = turn_of["values"]
            filled(act, "values")
            act.wait_ge(rstd_ready, norm["before_mix1"][1] + 1)
            for th in range(HALVES):
                ins = nc.scalar.activation(values[:, th, :], banks(turn)[:, th, :], ACT.Copy,
                                           scale=rstd_pre[:, T + th:T + th + 1])
            ins.then_inc(set_read[turn % 2], 1)
            for what, g in ATTENTION:
                turn = turn_of[what, g]
                if what == "q":
                    split_until(end[what, g] + AHEAD)
                    low_out((what, g))
                elif what == "scores":
                    seen.next(npeak_ready)
                    for i in range(HALVES * BANKS):
                        b, th = divmod(i, HALVES)
                        cols = slice(0, P) if th == 0 else slice(P, KEYS)
                        ins = nc.scalar.activation(probs[:, b, cols], masked[:, b, cols], ACT.Exp,
                                                   scale=SCALE, bias=npeak[:, i:i + 1], accum_out=total[:, i:i + 1])
                    ins.then_inc(exp_ready, 1)
                elif what == "T":
                    filled(act, (what, g))
                    nc.scalar.activation(probsT[:, :, :], banks(turn)[:, :, 0:KEYS], ACT.Copy).then_inc(set_read[turn % 2], 1)
                else:
                    filled(act, (what, g))
                    nc.scalar.activation(attended[:, BANKS * g:BANKS * g + BANKS, 0:T], banks(turn)[:, :, 0:T], ACT.Copy).then_inc(att_hi_ready, 1)
            for g in range(OUT_GROUPS):
                split_until(end["att_out", g] + AHEAD)
                low_out(("att_out", g))
                square_y(y_mix, "mixed1", g, turn_of["att_out", g])
            root("mixed1")
            residual(6 + 2, "before_cross1", ("cross_q", 1))
            cross_attention(1)
            ffn(1)

        @block.vector
        def _(dve):
            seen = Seen(dve)
            split = [0]
            v = nc.vector

            def step(ins):
                ins.then_inc(dve_step, 1)
                seen.next(dve_step)

            def split_lo(u0, j):
                slot = j % RING
                dve.wait_ge(hi_ready, u0 + (j + 1))
                v.tensor_tensor(w_lo[:, slot, :], raw[:, slot, :], w_hi[:, slot, :].bitcast(F32), ALU.subtract).then_inc(lo_ready, 1)

            def split_until(n):
                while split[0] < min(n, UNITS):
                    split_lo(split[0] // RING * RING, split[0] % RING)
                    split[0] += 1

            def add_low(out, turn, n=BANKS):
                seen.next(low_ready)
                v.tensor_tensor(out, banks(turn)[:, 0:n, 0:T], low[:, 0:n, :], ALU.add).then_inc(set_read[turn % 2], 1)
                read_out(dve, turn)

            def one_over_root(name):
                n = norm[name][1]
                w = T + HALVES if name in TOKEN_SUMS else T
                rstd = rstd_post if name == "mem" or name in MIXED else rstd_pre
                dve.wait_ge(std_ready, n + 1)
                v.reciprocal(rstd[:, 0:w], std[:, 0:w]).then_inc(rstd_ready, 1)
                dve.wait_ge(rstd_ready, n + 1)

            def add_squares(name, g):
                seen.next(y_squared)
                v.tensor_tensor(squares[:, :, :], squares[:, :, :], sq[:, :, :], ALU.add).then_inc(y_added, 1)
                seen.next(y_added)

            def x_low(src, gain, c, out):
                seen.next(x_hi_ready)
                v.scalar_tensor_tensor(out[:, c, T:2 * T], src[:, c, :], vec[:, gain, c:c + 1],
                                       out[:, c, 0:T].bitcast(F32), ALU.mult, ALU.subtract).then_inc(x_ready, 1)

            def residual(y, name, gain, first=None, units=FULL, next_gain=None):
                one_over_root(name)
                for c in range(0, C, BANKS):
                    step(v.tensor_tensor(y[:, c:c + BANKS, :], y[:, c:c + BANKS, :], over(rstd_post[:, 0:T], BANKS), ALU.mult))
                    for c in range(c, c + BANKS):
                        v.scalar_tensor_tensor(h[:, c, :], y[:, c, :], vec[:, gain, c:c + 1], h[:, c, :],
                                               ALU.mult, ALU.add).then_inc(h_ready, 1)
                        if next_gain is None:
                            continue
                        if c:
                            dve.wait_ge(h_ready, MIXED.index(name) * C + c)
                            x_low(h, next_gain, c - 1, X)
                        if c == C - 1:
                            dve.wait_ge(h_ready, MIXED.index(name) * C + C)
                            x_low(h, next_gain, c, X)
                        if c % 2 and units == FULL and c // 2 >= LAG:
                            split_until(start[first] + AHEAD + c // 2 - LAG + 1)

            def rotate(q, n):
                src, dst = q[0:ROT], swap[:, 0:n, :]
                step(v.stream_shuffle(dst, src, [(r + ROT // 2) % ROT for r in range(ROT)]))
                step(v.tensor_tensor(dst, dst, over(sin[:, :], n), ALU.mult))
                step(v.tensor_tensor(src, src, over(cos[:, :], n), ALU.mult))
                v.tensor_tensor(src, src, dst, ALU.add).then_inc(q_ready, 1)
                seen.next(q_ready)

            dve.wait_ge(consts_in, 32)
            for c in range(C):
                if c % 4 == 0:
                    dve.wait_ge(mem_in[c // 4], 16)
                x_low(mem, MEM_GAIN, c, XM)
                if c % 2:
                    split_until(c // 2 + 1 if c // 2 < AHEAD else AHEAD + max(0, c // 2 - LAG + 1))
            dve.wait_ge(pos_in, 16)
            step(v.tensor_copy(pos_f[:, :], pos_i[:, :]))
            step(v.tensor_scalar(ang[:, :], pos_f[:, :], const("inv")[0:ROT, :], None, ALU.mult))
            for n, quarter in enumerate((0.25, 0.0)):
                r = red[:, n, :]
                step(v.tensor_scalar(turns_[:, :], ang[:, :], float(1 / (2 * np.pi)), quarter, ALU.mult, ALU.add))
                step(v.tensor_scalar(turns_[:, :], turns_[:, :], ROUND, None, ALU.add))
                step(v.tensor_scalar(turns_[:, :], turns_[:, :], -ROUND, None, ALU.add))
                step(v.scalar_tensor_tensor(r, turns_[:, :], -TWO_PI_A, ang[:, :], ALU.mult, ALU.add))
                step(v.scalar_tensor_tensor(r, turns_[:, :], -TWO_PI_B, r, ALU.mult, ALU.add))
                step(v.scalar_tensor_tensor(r, turns_[:, :], -TWO_PI_C, r, ALU.mult, ALU.add))
                if quarter:
                    step(v.tensor_scalar(r, r, float(np.pi / 2), PI_BELOW, ALU.add, ALU.min))
                else:
                    step(v.tensor_scalar(r, r, PI_BELOW, None, ALU.min))
                step(v.tensor_scalar(r, r, -PI_BELOW, None, ALU.max))
            ins = v.tensor_scalar(red[:, 1, :], red[:, 1, :], const("sign")[0:ROT, :], None, ALU.mult)
            ins.then_inc(ang_ready, 1)
            def memory_keys(l):
                turn = turn_of["mem_keys", l]
                keys_out = (kv, kv1)[l][:, 0, :, :]
                add_low(keys_out, turn)
                v.tensor_tensor(keys_out, keys_out, over(rstd_post[:, 0:T], BANKS), ALU.mult).then_inc(mem_keys_out, 1)

            split_until(end["mem_keys", 0] + AHEAD)
            one_over_root("mem")
            memory_keys(0)
            split_until(end["mem_values", 0] + AHEAD)
            one_over_root("x")
            for c in range(C):
                step(v.scalar_tensor_tensor(xn[:, c, :], h[:, c, :], vec[:, 0, c:c + 1], rstd_pre[:, 0:T], ALU.mult, ALU.mult))
                if c % 2:
                    split_until(split[0] + 1)
            split_until(end["mem_keys", 1] + AHEAD)
            memory_keys(1)
            split_until(end["mem_values", 1] + AHEAD)
            dve.wait_ge(rope_ready, 2)
            for g, window in enumerate(POOL_WINDOWS):
                inp = xn[:, BANKS * g:BANKS * g + BANKS, :]
                src, w = inp, 1
                dst, other = (pool_b, pool_a) if window.bit_length() % 2 == 0 else (pool_a, pool_b)
                while w < window:
                    step(v.tensor_tensor(dst[:, :, w:T], src[:, :, w:T], src[:, :, 0:T - w], ALU.add))
                    step(v.tensor_copy(dst[:, :, 0:w], src[:, :, 0:w]))
                    src, w = dst, 2 * w
                    dst, other = other, dst
                edge = const("edge")[:, EDGE * g:EDGE * g + EDGE].unsqueeze(1).to_broadcast([P, BANKS, EDGE])
                step(v.tensor_tensor(src[:, :, 0:EDGE], src[:, :, 0:EDGE], edge, ALU.mult))
                step(v.tensor_tensor(pool_a[:, :, 0:EDGE], src[:, :, 0:EDGE], inp[:, :, 0:EDGE], ALU.subtract))
                v.scalar_tensor_tensor(pool_a[:, :, EDGE:T], src[:, :, EDGE:T], 1.0 / window, inp[:, :, EDGE:T],
                                       ALU.mult, ALU.subtract).then_inc(pooled, 1)
                dve.wait_ge(pooled, g + 1)
                seen.next(x_hi_ready)
                v.tensor_tensor(X[:, BANKS * g:BANKS * g + BANKS, T:2 * T], pool_a[:, :, :],
                                X[:, BANKS * g:BANKS * g + BANKS, 0:T].bitcast(F32), ALU.subtract).then_inc(x_ready, 1)
                dve.wait_ge(x_ready, C + g + 1)
            for g in range(OUT_GROUPS):
                split_until(end["pool", g] + AHEAD)
                if g == 0:
                    step(v.memset(squares[:, :, :], 0.0))
                turn = turn_of["pool", g]
                seen.next(low_ready)
                for b in range(BANKS):
                    c = BANKS * g + b
                    ins = v.scalar_tensor_tensor(y_mix[:, c, :], banks(turn)[:, b, 0:T], vec[:, POOL_SCALE, c:c + 1], low[:, b, :],
                                                 ALU.mult, ALU.add)
                ins.then_inc(set_read[turn % 2], 1)
                read_out(dve, turn)
                add_squares("mixed0", g)
            residual(y_mix, "mixed0", 1, ("cross_q", 0), next_gain=2)

            def normalise(p, n):
                step(v.reciprocal(rtotal[:, 0:n], total[:, 0:n]))
                for i in range(n):
                    ins = v.tensor_scalar(p(i), p(i), rtotal[:, i:i + 1], None, ALU.mult)
                ins.then_inc(probs_ready, 1)
                seen.next(probs_ready)

            def minus_peak():
                v.tensor_scalar(npeak[:, :], peak[:, :], -SCALE, None, ALU.mult).then_inc(npeak_ready, 1)

            def output_group(y, name, group, g):
                split_until(end[group] + AHEAD)
                if g == 0:
                    step(v.memset(squares[:, :, :], 0.0))
                add_low(y[:, BANKS * g:BANKS * g + BANKS, :], turn_of[group])
                add_squares(name, g)

            def cross_attention(l):
                split_until(end["cross_q", l] + AHEAD)
                one_over_root(f"before_cross{l}")
                add_low(xq[:, :, :], turn_of["cross_q", l])
                v.tensor_tensor(xq[:, :, :], xq[:, :, :], over(rstd_pre[:, 0:T], BANKS), ALU.mult).then_inc(q_ready, 1)
                seen.next(q_ready)
                turn = turn_of["cross_scores", l]
                filled(dve, ("cross_scores", l))
                step(v.reduce_max(peak[:, :], banks(turn).rearrange("p h (t m) -> p (h t) m", t=HALVES), AX_X))
                minus_peak()
                read_out(dve, turn)
                normalise(lambda i: xp[:, i // HALVES, i % HALVES, :], HALVES * X_HEADS)
                turn = turn_of["cross_o", l]
                seen.next(att_hi_ready)
                v.tensor_tensor(X[:, 0:X_HEADS, T:2 * T], banks(turn)[:, :, 0:T], X[:, 0:X_HEADS, 0:T].bitcast(F32),
                                ALU.subtract).then_inc(set_read[turn % 2], 1)
                for g in range(OUT_GROUPS):
                    output_group(y_mix, f"crossed{l}", ("cross_out", l, g), g)
                residual(y_mix, f"crossed{l}", 6 * l + 3, ("glu", l, 0), next_gain=6 * l + 4)

            def ffn(l):
                low_before = seen.count["low_ready"]

                def glu(turn, i, g):
                    dve.wait_ge(low_ready, i * 2 + (low_before + g + 1))
                    if l or g:
                        dve.wait_ge(hidden_ready, i * 2 + (l * GLU_GROUPS + g))
                    v.tensor_tensor(gu[:, :, :], banks(turn)[:, :, 0:T], low[:, :, :], ALU.add).then_inc(set_read[turn % 2], 1)
                    dve.wait_ge(set_read[turn % 2], i + (turn // 2 + 1))
                    v.tensor_tensor(gu[:, :, :], gu[:, :, :], over(rstd_pre[:, 0:T], BANKS), ALU.mult).then_inc(gu_scaled, 1)
                    dve.wait_ge(gu_scaled, i * 2 + (l * GLU_GROUPS + g + 1))
                    dve.wait_ge(silu_ready, i * 2 + (l * GLU_GROUPS + g + 1))
                    v.tensor_tensor(hid[:, :, :], act_gate[:, :, :], gu[:, 2:4, :], ALU.mult).then_inc(hid_ready, 1)
                    dve.wait_ge(hid_ready, i * 2 + (l * GLU_GROUPS + g + 1))
                    dve.wait_ge(hid_hi_ready, i * 2 + (l * GLU_GROUPS + g + 1))
                    v.tensor_tensor(hidden[:, bass.ds(i * 4 + 2 * g, 2), T:2 * T], hid[:, :, :],
                                    hidden[:, bass.ds(i * 4 + 2 * g, 2), 0:T].bitcast(F32), ALU.subtract).then_inc(hidden_ready, 1)

                for g in range(2):
                    split_until(end["glu", l, g] + AHEAD)
                    if g == 0:
                        one_over_root(f"before_ffn{l}")
                    glu(turn_of["glu", l, g], 0, g)
                with dve.Fori(0, GLU_GROUPS // 2 - 1) as i:
                    for k in range(2):
                        for j in range(FULL):
                            split_lo(i * (2 * FULL) + split[0], FULL * k + j)
                        glu(turn_of["glu", l, 2 + k], i, 2 + k)
                split[0] += (GLU_GROUPS - 2) * FULL
                seen.count["low_ready"] += GLU_GROUPS
                dve.wait_ge(hidden_ready, (l + 1) * GLU_GROUPS)
                for g in range(OUT_GROUPS):
                    output_group(y_ffn, f"ffn{l}", ("down", l, g), g)

            cross_attention(0)
            ffn(0)
            residual(y_ffn, "ffn0", 5, units=IDX_UNITS, next_gain=6)

            split_until(end["idx"] + AHEAD)
            one_over_root("before_mix1")
            turn = turn_of["idx"]
            filled(dve, "idx")
            for th in range(HALVES):
                step(v.tensor_scalar(iw[:, th, :], banks(turn)[:, 1 + th, 0:IDX_HEADS], rstd_pre[:, T + th:T + th + 1], IW_SCALE,
                                     ALU.mult, ALU.mult))
            add_low(ik[:, :].unsqueeze(1), turn, 1)
            step(v.tensor_tensor(ik[:, :], ik[:, :], rstd_pre[:, 0:T], ALU.mult))
            rotate(ik[:, :].unsqueeze(1), 1)

            def heads_out(q, name):
                split_until(end[name] + AHEAD)
                add_low(q[:, :, :], turn_of[name])
                step(v.tensor_tensor(q[:, :, :], q[:, :, :], over(rstd_pre[:, 0:T], BANKS), ALU.mult))
                rotate(q, BANKS)

            def taking(rounds):
                for _ in range(rounds):
                    for th, cols in enumerate((slice(0, P), slice(P, KEYS))):
                        step(v.max(top8[:, th, :], work[:, cols]))
                        step(v.match_replace(work[:, cols], top8[:, th, :], work[:, cols], TAKEN))

            step(v.memset(score[:, :], 0.0))
            for g in range(5):
                heads_out(quad[g % 2] if g < 4 else keys, ("iq", g) if g < 4 else "keys")
                if g:
                    read_out(dve, turn_of["logits", g - 1])
                    for b in range(BANKS):
                        for th, cols in enumerate((slice(0, P), slice(P, KEYS))):
                            hd = BANKS * (g - 1) + b
                            ins = v.scalar_tensor_tensor(score[:, cols], masked[:, b, cols], iw[:, th, hd:hd + 1], score[:, cols],
                                                         ALU.mult, ALU.add)
                            if th == 1 and b == BANKS - 1:
                                ins.then_inc(scores_added, 1)
                                seen.next(scores_added)
                            else:
                                step(ins)
            step(v.tensor_tensor(work[:, :], score[:, :], causal, ALU.add))
            taking(4)
            split_until(end["values"] + AHEAD)
            taking(TOPK // 8 - 4)
            step(v.tensor_scalar(mask[:, :], work[:, :], TAKEN_BELOW, NEG, ALU.is_gt, ALU.mult))
            step(v.tensor_tensor(mask[:, :], mask[:, :], causal, ALU.add))
            for what, g in ATTENTION:
                turn = turn_of[what, g]
                if what == "q":
                    heads_out(quad[g % 2], (what, g))
                elif what == "scores":
                    filled(dve, (what, g))
                    for i in range(HALVES * BANKS):
                        b, th = divmod(i, HALVES)
                        cols = slice(0, P) if th == 0 else slice(P, KEYS)
                        ins = v.tensor_tensor_reduce(masked[:, b, cols], banks(turn)[:, b, cols], mask[:, cols], 1.0, TAKEN,
                                                     ALU.add, ALU.max, peak[:, i:i + 1])
                    ins.then_inc(set_read[turn % 2], 1)
                    read_out(dve, turn)
                    minus_peak()
                    seen.next(exp_ready)
                    normalise(lambda i: probs[:, i // HALVES, slice(0, P) if i % HALVES == 0 else slice(P, KEYS)], HALVES * BANKS)
                elif what == "o":
                    seen.next(att_hi_ready)
                    out = attended[:, BANKS * g:BANKS * g + BANKS]
                    v.tensor_tensor(out[:, :, T:2 * T], banks(turn)[:, :, 0:T], out[:, :, 0:T].bitcast(F32),
                                    ALU.subtract).then_inc(set_read[turn % 2], 1)
            for g in range(OUT_GROUPS):
                output_group(y_mix, "mixed1", ("att_out", g), g)
            residual(y_mix, "mixed1", 6 + 1, ("cross_q", 1), next_gain=6 + 2)
            cross_attention(1)
            ffn(1)
            residual(y_ffn, "ffn1", 6 + 5)

        @block.tensor
        def _(pe):
            seen = Seen(pe)
            mm = nc.tensor.matmul

            def set_free(turn, i=0):
                if turn >= 2:
                    pe.wait_ge(set_read[turn % 2], i + turn // 2)

            def sum_squares(name):
                turn, n = norm[name]
                out = banks(turn)[:, BANKS - 1, :]
                set_free(turn)
                if name in MIXED:
                    pe.wait_ge(y_added, (MIXED.index(name) + 1) * OUT_GROUPS)
                    for b in range(BANKS):
                        ins = mm(out[:, 0:T], ones, squares[:, b, :], start=b == 0, stop=b == BANKS - 1)
                else:
                    pe.wait_ge(h_added, (SUMS.index(name) + 1) * C)
                    ins = mm(out[:, 0:T], ones, hsum[:, :], start=True, stop=True)
                if name in TOKEN_SUMS:
                    for th in range(HALVES):
                        ins = mm(out[:, T + th:T + th + 1], hsum[:, th * P:th * P + P], ones[:, 0:1], start=True, stop=True)
                ins.then_inc(ss_ready, 1)

            def group(turn, u0, units, x, x_wait=None, after_sum=None, i=0, unit_step=0):
                set_free(turn, i)
                out = banks(turn)
                for j in range(units):
                    pe.wait_ge(lo_ready, (i * unit_step if unit_step else 0) + (u0 + j + 1))
                    slot = (u0 + j) % RING
                    for kk in range(2):
                        k = 2 * j + kk
                        if x_wait:
                            x_wait(k)
                        for b in range(BANKS):
                            if after_sum and k == 0 and b == BANKS - 1:
                                pe.wait_ge(std_ready, norm[after_sum][1] + 1)
                            w = slice(kk * BANKS * P + b * P, kk * BANKS * P + b * P + P)
                            last = k == 2 * units - 1
                            mm(out[:, b, :], w_hi[:, slot, w], x(k), start=k == 0, stop=False)
                            ins = mm(out[:, b, T:2 * T], w_lo[:, slot, w], x(k)[:, 0:T], start=False, stop=last)
                    ins.then_inc(units_used, 1)

            def named(name, x, x_wait=None, after_sum=None):
                group(turn_of[name], start[name], end[name] - start[name], x, x_wait, after_sum)

            def tokens_product(out, x, w_h, w_l, first, last):
                for th in range(HALVES):
                    o = out(th)
                    hi = x[:, th * P:th * P + P]
                    mm(o, hi, w_h, start=first, stop=False)
                    mm(o, hi, w_l, start=False, stop=False)
                    ins = mm(o, x[:, T + th * P:T + th * P + P], w_h, start=False, stop=last)
                return ins

            def token_group(name, x):
                turn = turn_of[name]
                set_free(turn)
                for j in range(FULL):
                    u = start[name] + j
                    pe.wait_ge(lo_ready, u + 1)
                    for kk in range(2):
                        k = 2 * j + kk
                        w = slice(kk * BANKS * P, (kk + 1) * BANKS * P)
                        ins = tokens_product(lambda th: banks(turn)[:, th, :], x(k), w_hi[:, u % RING, w], w_lo[:, u % RING, w],
                                             k == 0, k == C - 1)
                    ins.then_inc(units_used, 1)

            def in_X(k):
                return X[:, k, :]

            def in_XM(k):
                return XM[:, k, :]

            def next_x(k):
                seen.next(x_ready)

            pe.wait_ge(consts_in, 32)
            named(("mem_keys", 0), in_XM, next_x)
            sum_squares("mem")
            pe.wait_ge(std_ready, 1)
            token_group(("mem_values", 0), in_XM)
            sum_squares("x")
            named(("mem_keys", 1), in_XM, after_sum="x")
            token_group(("mem_values", 1), in_XM)
            for g in range(OUT_GROUPS):
                seen.next(x_ready)
                named(("pool", g), lambda k: X[:, BANKS * g + k, :])
            sum_squares("mixed0")

            def cross_attention(l):
                named(("cross_q", l), in_X, next_x)
                sum_squares(f"before_cross{l}")
                if l:
                    pe.wait_ge(kv_loaded, 16)
                turn = turn_of["cross_scores", l]
                seen.next(q_ready)
                for hd in range(X_HEADS):
                    for th in range(HALVES):
                        ins = mm(banks(turn)[:, hd, th * T:th * T + T], xq[:, hd, th * P:th * P + P], kv[:, 0, hd, :], start=True, stop=True)
                ins.then_inc(psum_filled, 1)
                turn = turn_of["cross_T", l]
                set_free(turn)
                seen.next(probs_ready)
                for hd in range(X_HEADS):
                    for m in range(2):
                        for th in range(HALVES):
                            ins = nc.tensor.transpose(banks(turn)[:, hd, m * T + th * P:m * T + th * P + P],
                                                      xp[:, hd, th, m * P:m * P + P], ident)
                ins.then_inc(psum_filled, 1)
                turn = turn_of["cross_o", l]
                set_free(turn)
                read_out(pe, turn_of["cross_T", l])
                for hd in range(X_HEADS):
                    for m in range(2):
                        ins = mm(banks(turn)[:, hd, 0:T], kv[:, 1, 2 * m + hd // 2, hd % 2 * P:hd % 2 * P + P], xpT[:, hd, m, :],
                                 start=m == 0, stop=m == 1)
                ins.then_inc(psum_filled, 1)
                read_out(pe, turn)
                for g in range(OUT_GROUPS):
                    named(("cross_out", l, g), in_X)
                sum_squares(f"crossed{l}")

            def ffn(l):
                named(("glu", l, 0), in_X, next_x)
                sum_squares(f"before_ffn{l}")
                named(("glu", l, 1), in_X, after_sum=f"before_ffn{l}")
                with pe.Fori(0, GLU_GROUPS // 2 - 1) as i:
                    for k in range(2):
                        group(turn_of["glu", l, 2 + k], start["glu", l, 2 + k], FULL, in_X, i=i, unit_step=2 * FULL)

                def hidden_there(k):
                    if k % 2 == 0:
                        pe.wait_ge(hidden_ready, l * GLU_GROUPS + k // 2 + 1)

                with pe.Fori(0, OUT_GROUPS // 2) as i:
                    for k in range(2):
                        group(turn_of["down", l, k], start["down", l, k], DOWN, lambda c: hidden[:, c, :],
                              hidden_there if k == 0 else None, i=i, unit_step=2 * DOWN)
                sum_squares(f"ffn{l}")

            cross_attention(0)
            ffn(0)

            turn = turn_of["idx"]
            set_free(turn)
            pe.wait_ge(std_ready, norm["ffn0"][1] + 1)
            for j in range(IDX_UNITS):
                u = start["idx"] + j
                pe.wait_ge(lo_ready, u + 1)
                for kk in range(4):
                    k = 4 * j + kk
                    seen.next(x_ready)
                    w = slice(kk * 2 * P, kk * 2 * P + P)
                    mm(banks(turn)[:, 0, :], w_hi[:, u % RING, w], X[:, k, :], start=k == 0, stop=False)
                    mm(banks(turn)[:, 0, T:2 * T], w_lo[:, u % RING, w], X[:, k, 0:T], start=False, stop=k == C - 1)
                    w = slice(kk * 2 * P + P, kk * 2 * P + P + IDX_HEADS)
                    ins = tokens_product(lambda th: banks(turn)[:, 1 + th, 0:IDX_HEADS], X[:, k, :], w_hi[:, u % RING, w],
                                         w_lo[:, u % RING, w], k == 0, k == C - 1)
                ins.then_inc(units_used, 1)
            sum_squares("before_mix1")

            def query_key(turn, q, k):
                for b in range(BANKS):
                    mm(banks(turn)[:, b, 0:P], q[:, b, 0:P], k[:, 0:P], start=True, stop=True)
                    ins = mm(banks(turn)[:, b, P:KEYS], q[:, b, P:T], k, start=True, stop=True)
                ins.then_inc(psum_filled, 1)

            seen.next(q_ready)
            for g in range(5):
                name = ("iq", g) if g < 4 else "keys"
                named(name, in_X, after_sum="before_mix1" if g == 0 else None)
                if g:
                    turn = turn_of["logits", g - 1]
                    set_free(turn)
                    seen.next(q_ready)
                    query_key(turn, quad[(g - 1) % 2], ik[:, :])
            seen.next(q_ready)
            token_group("values", in_X)
            for what, g in ATTENTION:
                turn = turn_of[what, g]
                if what == "q":
                    named((what, g), in_X)
                elif what == "scores":
                    set_free(turn)
                    seen.next(q_ready)
                    query_key(turn, quad[g % 2], keys[:, g, :])
                elif what == "T":
                    set_free(turn)
                    seen.next(probs_ready)
                    for b in range(BANKS):
                        for n in range(KEYS // P):
                            ins = nc.tensor.transpose(banks(turn)[:, b, n * P:n * P + P], probs[:, b, n * P:n * P + P], ident)
                    ins.then_inc(psum_filled, 1)
                else:
                    set_free(turn)
                    read_out(pe, turn_of["T", g])
                    if g == 0:
                        read_out(pe, turn_of["values"])
                    for b in range(BANKS):
                        mm(banks(turn)[:, b, 0:T], values[:, 0, g * P:g * P + P], probsT[:, b, 0:T], start=True, stop=False)
                        ins = mm(banks(turn)[:, b, P:T], values[:, 1, g * P:g * P + P], probsT[:, b, T:KEYS], start=False, stop=True)
                    ins.then_inc(psum_filled, 1)
            read_out(pe, turn_of["o", 3])
            read_out(pe, turn_of["o", 2])
            for g in range(OUT_GROUPS):
                named(("att_out", g), lambda k: attended[:, k, :])
            sum_squares("mixed1")
            cross_attention(1)
            ffn(1)


def _units(w):
    k = w.shape[0] // (2 * P)
    return w.reshape(k, 2, P, BANKS * P).transpose(0, 2, 1, 3).reshape(k, P, UNIT)


def kernel(**inputs):
    import concourse.bacc as bacc
    from concourse.bass_utils import run_bass_kernel_spmd

    a = {k: np.asarray(v) for k, v in inputs.items()}
    w_in, w_out = a["dsa_w_in"][0], a["dsa_w_out"][0]
    edges = np.cumsum([0, HEADS * P, KV_HEADS * P, KV_HEADS * P, IDX_HEADS * P, P, IDX_HEADS])
    q, k, v, iq, ik, iw = (w_in[:, x:y] for x, y in zip(edges, edges[1:]))
    W = BANKS * P
    stream = np.empty((UNITS, P, UNIT), np.float32)
    plan = Plan()
    for name, n in plan.weights:
        at = plan.start[name]
        kind, l, g = (tuple(name) if isinstance(name, tuple) else (name,)) + (None,) * (3 - (len(name) if isinstance(name, tuple) else 1))
        cols = lambda w, g: w[:, g * W:(g + 1) * W]
        if kind == "idx":
            both = np.concatenate([ik, iw, np.zeros((D, 2 * P - P - IDX_HEADS), np.float32)], 1)
            stream[at:at + n] = both.reshape(n, 4, P, 2 * P).transpose(0, 2, 1, 3).reshape(n, P, UNIT)
            continue
        if kind == "mem_keys":
            w = cols(a["xattn_wkv"][l], 0)
        elif kind == "mem_values":
            w = cols(a["xattn_wkv"][l], 1)
        elif kind == "pool":
            w = a["pool_w"][0, l]
        elif kind == "cross_q":
            w = a["xattn_wq"][l]
        elif kind == "cross_out":
            w = cols(a["xattn_wo"][l], g)
        elif kind == "glu":
            gate = a["ffn_w_gate_up"][l][:, 2 * P * g:2 * P * (g + 1)]
            up = a["ffn_w_gate_up"][l][:, D_FF + 2 * P * g:D_FF + 2 * P * (g + 1)]
            w = np.concatenate([gate, up], 1)
        elif kind == "down":
            w = cols(a["ffn_w_down"][l], g)
        elif kind == "iq":
            w = cols(iq, l)
        elif kind == "q":
            w = cols(q, l)
        elif kind == "keys":
            w = k
        elif kind == "values":
            w = v
        else:
            w = cols(w_out, l)
        stream[at:at + n] = _units(w)

    def by_feature(x):
        return np.ascontiguousarray(x.T.reshape(C, P, x.shape[0]).transpose(1, 0, 2))

    gains = np.concatenate([a["norm_gains"].reshape(6 * LAYERS, D), a["mem_norm"][None], a["pool_scale"]])
    vectors = np.ascontiguousarray(gains.reshape(N_GAINS, C, P).transpose(2, 0, 1))
    consts = np.zeros((P, N_CONST), np.float32)
    put = lambda name, x: consts.__setitem__((slice(0, x.shape[0]), slice(CONST_AT[name], CONST_AT[name] + CONST[name])), x)
    put("ident", np.eye(P, dtype=np.float32))
    put("ones", np.ones((P, P), np.float32))
    query, key = np.arange(P)[:, None], np.arange(T)[None]
    put("causal", np.concatenate([np.where(key[:, :P] <= query, 0, NEG), np.where(key <= query + P, 0, NEG)], 1).astype(np.float32))
    edge = [1 / np.minimum(np.arange(EDGE) + 1, w) for w in POOL_WINDOWS]
    put("edge", np.broadcast_to(np.concatenate(edge).astype(np.float32), (P, CONST["edge"])))
    inv = np.float32(500000.0) ** (-np.arange(0, ROT, 2, dtype=np.float32) / np.float32(ROT))
    put("inv", np.concatenate([inv, inv])[:, None])
    put("sign", np.concatenate([-np.ones(ROT // 2), np.ones(ROT // 2)])[:, None].astype(np.float32))
    put("eps", np.full((P, 1), EPS, np.float32))
    arrays = {
        "xT": by_feature(a["x"][0]), "memT": by_feature(a["mem"][0]), "positions": np.ascontiguousarray(a["positions"], np.int32),
        "vectors": vectors, "constants": consts, "weights": stream,
    }
    nc = bacc.Bacc("TRN2", target_bir_lowering=False, num_devices=1)
    args = [nc.dram_tensor(n, x.shape, mybir.dt.from_np(x.dtype), kind="ExternalInput").ap() for n, x in arrays.items()]
    out = nc.dram_tensor("outT", (P, C, T), F32, kind="ExternalOutput").ap()
    kv_store = nc.dram_tensor("kv_store", (P, 2, BANKS, T), F32, kind="Internal").ap()
    hybrid_trunk(nc, *args, out, kv_store)
    result = run_bass_kernel_spmd(nc, [arrays], core_ids=[0])
    got = result.results[0]["outT"]
    return np.ascontiguousarray(got.transpose(2, 1, 0).reshape(1, T, D))
```

```python
import numpy as np
import concourse.bass as bass
from concourse import mybir
from contextlib import ExitStack

F32 = mybir.dt.float32
F32R = mybir.dt.float32r
I32 = mybir.dt.int32
ALU = mybir.AluOpType
ACT = mybir.ActivationFunctionType
AX_X = mybir.AxisListType.X

P = 128
T = 256
HALVES = T // P
D = 2048
C = D // P
D_FF = 5632
CF = D_FF // P
LAYERS = 2
POOL_WINDOWS = (2, 4, 8, 16)
REACH = P + max(POOL_WINDOWS)
HEADS, KV_HEADS, IDX_HEADS, X_HEADS = 16, 4, 16, 4
ROT = P // 4
TOPK = T // 4
EPS = 1e-6
SCALE = float(P) ** -0.5
IW_SCALE = float(IDX_HEADS) ** -0.5
NEG = -1e30
TAKEN = -3e38
TAKEN_BELOW = -2e38

UNIT = 1024
RING = 4
AHEAD = 4
LAG = 1
MEM_PARTS = C // 2
BANKS = 4
FULL = C // 2
PAIR = 2
DOWN = CF // 2
GLU_GROUPS = D_FF // (2 * P)
OUT_GROUPS = C // BANKS
IDX_UNITS = C // 4
UNITS = (4 * FULL + OUT_GROUPS * PAIR + LAYERS * (FULL + OUT_GROUPS * PAIR + GLU_GROUPS * FULL + OUT_GROUPS * DOWN)
         + IDX_UNITS + 10 * FULL + OUT_GROUPS * FULL)

N_GAINS = 6 * LAYERS + 2
MEM_GAIN, POOL_SCALE = 6 * LAYERS, 6 * LAYERS + 1
KEYS = P + T
CONST = {"ident": P, "ones": P, "causal": KEYS, "inv": 1, "sign": 1, "eps": 1}
CONST_AT = dict(zip(CONST, np.cumsum([0] + list(CONST.values()))))
N_CONST = sum(CONST.values())

TWO_PI_A = 6.28125
TWO_PI_B = float(np.float32(np.round((2 * np.pi - TWO_PI_A) * 2**21) / 2**21))
TWO_PI_C = float(np.float32(2 * np.pi - TWO_PI_A - TWO_PI_B))
ROUND = 1.5 * 2.0**23
PI_BELOW = 3.1415925



class Plan:

    def __init__(self):
        self.place, self.start, self.end, self.units, self.norm = {}, {}, {}, 0, {}
        self.in_set, self.last, self.pending, self.sum_before = [0, 0], 1, {}, {}
        self.set_before = {}
        self.filled = {}
        self.weights = []
        self.group(("mem_keys", 0), FULL)
        self.sum_squares("mem")
        self.turn(("means", 0))
        self.group(("mem_values", 0), FULL)
        self.turn(("means", 1))
        for g in range(OUT_GROUPS):
            self.group(("pool", g), PAIR)
        self.group(("mem_values", 1), FULL)
        self.sum_squares("mixed0")
        self.group(("cross_q", 0), FULL)
        self.sum_squares("before_cross0")
        self.group(("mem_keys", 1), FULL)
        self.cross(0)
        self.ffn(0)
        self.group("idx", IDX_UNITS)
        self.sum_squares("before_mix1")
        for name in SPARSE:
            self.group(name, FULL)
            for _, turn in BESIDE.get(name, ()):
                self.turn(turn, beside=True)
        for g in range(1, OUT_GROUPS):
            self.group(("att_out", g), FULL)
        self.sum_squares("mixed1")
        self.group(("cross_q", 1), FULL)
        self.sum_squares("before_cross1")
        self.cross(1)
        self.ffn(1)
        assert self.units == UNITS

    def _put(self, name, beside=False):
        which = 1 - self.last
        self.place[name] = which, self.in_set[which]
        self.in_set[which] += 1
        if beside:
            return
        self.last = which
        if self.last in self.pending:
            self.sum_before[name] = self.pending.pop(self.last)

    def group(self, name, units):
        self._put(name)
        self.start[name] = self.units
        self.units += units
        self.end[name] = self.units
        self.weights.append((name, units))

    def turn(self, name, beside=False):
        self._put(name, beside)
        self.filled[name] = len(self.filled) + 1

    def sum_squares(self, name):
        self.norm[name] = 1 - self.last, len(self.norm)
        self.set_before[name] = self.in_set[1 - self.last]
        self.pending[1 - self.last] = name

    def cross(self, l):
        self._put(("cross", l))
        for g in range(OUT_GROUPS):
            self.group(("cross_out", l, g), PAIR)
        self.sum_squares(f"crossed{l}")

    def ffn(self, l):
        self.group(("glu", l, 0), FULL)
        self.sum_squares(f"before_ffn{l}")
        for g in range(1, GLU_GROUPS):
            self.group(("glu", l, g), FULL)
        for g in range(OUT_GROUPS):
            self.group(("down", l, g), DOWN)
        self.sum_squares(f"ffn{l}")


SPARSE = tuple(("iq", g) for g in range(4)) + ("keys", "values") + tuple(("q", g) for g in range(4)) + (("att_out", 0),)
BESIDE = {
    ("iq", 1): ((5, ("logits", 0)),), ("iq", 2): ((5, ("logits", 1)),), ("iq", 3): ((5, ("logits", 2)),),
    "keys": ((5, ("logits", 3)),), ("q", 1): ((5, ("scores", 0)),),
    ("q", 2): ((1, ("T", 0)), (3, ("o", 0)), (5, ("scores", 1))),
    ("q", 3): ((1, ("T", 1)), (3, ("o", 1)), (5, ("scores", 2))),
    ("att_out", 0): ((1, ("T", 2)), (2, ("o", 2)), (4, ("scores", 3)), (6, ("T", 3)), (6, ("o", 3))),
}
SUMS = ("mem", "before_cross0", "before_ffn0", "before_mix1", "before_cross1", "before_ffn1")
ROW_SUMS = ("mem", "before_ffn0", "before_mix1", "before_ffn1", "mixed0", "crossed0", "ffn0", "mixed1", "crossed1", "ffn1")
TOKEN_SUMS = ("mem", "before_cross0", "before_mix1", "before_cross1")
Y_ADDED = OUT_GROUPS
Y_SQUARED = OUT_GROUPS - 1 + BANKS
DVE_SCALES = BANKS
POOL_LEAD = 2
CROSS = (("s", 0), ("s", 1), ("s", 2), ("s", 3), ("T", 0), ("T", 1), ("T", 2), ("T", 3), ("o", 0), ("o", 1), ("o", 2), ("o", 3))
MIXED = ("mixed0", "crossed0", "ffn0", "mixed1", "crossed1", "ffn1")


class Seen:

    def __init__(self, eng):
        self.eng, self.count = eng, {}

    def next(self, sem, k=1):
        self.count[sem.name] = self.count.get(sem.name, 0) + k
        self.eng.wait_ge(sem, self.count[sem.name])


def hybrid_trunk(nc, xT, x_tokens, memT, positions, averages, vectors, constants, weights, outT, kv_store):
    plan = Plan()
    place_of, start, end, norm = plan.place, plan.start, plan.end, plan.norm
    ctx = ExitStack()
    with ctx:
        at = [(nc.sbuf_base + 31) // 32 * 32]

        def place(name, shape, dt, offset=None):
            size = int(np.prod(shape[1:])) * 4
            if offset is None:
                offset = at[0]
                at[0] += (size + 31) // 32 * 32
            return nc.alloc_sbuf_tensor_at(name, shape, dt, offset=offset)

        def sem(name):
            return ctx.enter_context(nc.semaphore(name))

        K = 1024
        h = place("h", [P, C, T], F32)
        x_at = at[0]
        X = place("X", [P, C, 2 * T], F32R)
        raw = place("raw", [P, RING, UNIT], F32)
        w_hi = place("w_hi", [P, RING, UNIT], F32R)
        w_lo = place("w_lo", [P, RING, UNIT], F32R)
        low = place("low", [P, BANKS, T], F32)
        gu = place("gu", [P, BANKS, T], F32)
        sq = gu
        tail = at[0]
        squares = place("squares", [P, BANKS, T], F32)
        act_gate = place("act_gate", [P, 2, T], F32, tail)
        hid = place("hid", [P, 2, T], F32, tail + 2 * K)
        consts = place("consts", [P, N_CONST], F32)
        vec = place("vec", [P, N_GAINS, C], F32)
        x_square = place("x_square", [P, HALVES, D], F32, x_at)
        std = place("std", [P, T + HALVES], F32)
        rstd_post = place("rstd_post", [P, T], F32)
        rstd_pre = place("rstd_pre", [P, T + HALVES], F32)
        rstd_mem = place("rstd_mem", [P, T + HALVES], F32)
        hsum = place("hsum", [P, T], F32)
        cos = place("cos", [ROT, T], F32)
        sin = place("sin", [ROT, T], F32)
        iw = place("iw", [P, HALVES, IDX_HEADS], F32)
        x_rstd = place("x_rstd", [P, 3, HALVES], F32)
        cross_scale = place("cross_scale", [P, 2, HALVES], F32)
        warm = place("warm", [P, 32], F32)
        peak = place("peak", [P, 8], F32)
        npeak = place("npeak", [P, 8], F32)
        total = place("total", [P, 8], F32)
        rtotal = place("rtotal", [P, 8], F32)
        top8 = place("top8", [P, HALVES, 8], F32)

        base = at[0]
        at[0] += CF * 2 * K
        assert at[0] <= nc.sbuf_usable_end, (at[0], nc.sbuf_usable_end)
        hidden = place("hidden", [P, CF, 2 * T], F32R, base)
        y_mix = place("y_mix", [P, C, T], F32, base + 64 * K)
        y_ffn = place("y_ffn", [P, C, T], F32, x_at + 16 * K)
        kv = place("kv", [P, 2, BANKS, T], F32, base + 80 * K)
        XM = place("XM", [P, C, 2 * T], F32R, base)
        kv1 = place("kv1", [P, 2, BANKS, T], F32, base + 32 * K)
        average = place("average", [P, len(POOL_WINDOWS), REACH + P], F32, base + 40 * K)
        mem = place("mem", [P, C, T], F32, base + 48 * K)
        x_tok = place("x_tok", [P, HALVES, D], F32, base + 64 * K)
        ang = place("ang", [ROT, T], F32, base + 32 * K)
        turns_ = place("turns", [ROT, T], F32, base + 33 * K)
        red = place("red", [ROT, 2, T], F32, base + 34 * K)
        pos_i = place("pos_i", [ROT, T], I32, base + 36 * K)
        pos_f = place("pos_f", [ROT, T], F32, base + 37 * K)
        xq = place("xq", [P, X_HEADS, T], F32, base + 40 * K)
        xp = place("xp", [P, X_HEADS, HALVES, T], F32, base + 44 * K)
        xpT = place("xpT", [P, X_HEADS, HALVES, T], F32, base + 52 * K)
        quad = [place(f"quad{n}", [P, BANKS, T], F32, base + 4 * K * n) for n in range(2)]
        keys = place("keys", [P, KV_HEADS, T], F32, base + 8 * K)
        values = place("values", [P, HALVES, KV_HEADS * P], F32, base + 12 * K)
        ik = place("ik", [P, T], F32, base + 16 * K)
        score = place("score", [P, KEYS], F32, base + 17 * K)
        work = place("work", [P, KEYS], F32, base + 18 * K + 512)
        mask = place("mask", [P, KEYS], F32, base + 20 * K)
        swap = place("swap", [ROT, BANKS, T], F32, base + 21 * K + 512)
        masked = place("masked", [P, BANKS, KEYS], F32, base + 26 * K)
        attended = place("attended", [P, HEADS, 2 * T], F32R, base + 32 * K)
        probs = place("probs", [P, BANKS, KEYS], F32, base + 64 * K)
        probsT = place("probsT", [P, BANKS, KEYS], F32, base + 70 * K)

        ps = ctx.enter_context(nc.psum_tensor("ps", [P, 2 * BANKS, 2 * T], F32))

        def const(name):
            return consts[:, CONST_AT[name]:CONST_AT[name] + CONST[name]]

        def bank_set(n):
            return ps[:, BANKS * n:BANKS * n + BANKS, :]

        def banks(name):
            return bank_set(place_of[name][0])

        def means_at(c):
            return banks(("means", c // 8))[:, c % 8 // 2, c % 2 * T:c % 2 * T + T]

        probs_before = 0, X_HEADS + 2 * (HEADS // BANKS)

        def over(row, n):
            return row.unsqueeze(1).to_broadcast([row.shape[0], n, T])

        ident, ones, causal = const("ident"), const("ones"), const("causal")

        landed = [sem(f"landed{n}") for n in range(RING)]
        hi_ready = sem("hi_ready")
        lo_ready = sem("lo_ready")
        units_used = sem("units_used")
        psum_filled = sem("psum_filled")
        set_read = [sem(f"set_read{n}") for n in range(2)]
        low_ready = sem("low_ready")
        bank_filled = sem("bank_filled")
        y_ready = sem("y_ready")
        y_squared = sem("y_squared")
        y_added = sem("y_added")
        ss_ready = sem("ss_ready")
        std_ready = sem("std_ready")
        x_squared = sem("x_squared")
        x_std_ready = sem("x_std_ready")
        x_normed = sem("x_normed")
        y_scaled = sem("y_scaled")
        h_ready = sem("h_ready")
        h_squared = sem("h_squared")
        h_added = sem("h_added")
        x_hi_ready = sem("x_hi_ready")
        x_ready = sem("x_ready")
        q_ready = sem("q_ready")
        relu_ready = sem("relu_ready")
        npeak_ready = sem("npeak_ready")
        scores_added = sem("scores_added")
        exp_ready = sem("exp_ready")
        probs_ready = sem("probs_ready")
        att_hi_ready = sem("att_hi_ready")
        att_ready = sem("att_ready")
        mem_values_out = sem("mem_values_out")
        mem_keys_out = sem("mem_keys_out")
        rstd_ready = sem("rstd_ready")
        gu_scaled = sem("gu_scaled")
        silu_ready = sem("silu_ready")
        hid_ready = sem("hid_ready")
        hid_hi_ready = sem("hid_hi_ready")
        hidden_ready = sem("hidden_ready")
        scale_ready = sem("scale_ready")
        head_filled = sem("head_filled")
        head_T = sem("head_T")
        ang_ready = sem("ang_ready")
        rope_ready = sem("rope_ready")
        dve_step = sem("dve_step")
        consts_in = sem("consts_in")
        pos_in = sem("pos_in")
        mem_in = [sem(f"mem_in{n}") for n in range(MEM_PARTS)]
        x_in = sem("x_in")
        x_tok_in = [sem(f"x_tok_in{n}") for n in range(HALVES)]
        average_in = sem("average_in")
        kv_stored = sem("kv_stored")
        kv_loaded = sem("kv_loaded")
        out_done = sem("out_done")

        block = ctx.enter_context(nc.Block())

        def filled(eng, name):
            if name in end:
                eng.wait_ge(units_used, end[name])
            else:
                eng.wait_ge(psum_filled, plan.filled[name])

        def read_out(eng, name):
            which, n = place_of[name]
            eng.wait_ge(set_read[which], n + 1)

        def read_signal(name):
            return set_read[place_of[name][0]]

        @block.sync
        def _(sp):
            for n in range(MEM_PARTS):
                sp.dma_start(mem[:, 2 * n:2 * n + 2, :], memT[:, 2 * n:2 * n + 2, :]).then_inc(mem_in[n], 16)
                if n < RING:
                    sp.dma_start(raw[:, n, :], weights[n]).then_inc(landed[n], 16)
            with sp.Fori(0, UNITS // RING - 1) as i:
                for n in range(RING):
                    sp.wait_ge(lo_ready, i * RING + (n + 1))
                    sp.dma_start(raw[:, n, :], weights[bass.ds(i * RING + (RING + n), 1)].squeeze(0)).then_inc(landed[n], 16)
            for n in range(4):
                sp.wait_ge(h_ready, C * (len(MIXED) - 1) + 4 * n + 4)
                sp.dma_start(outT[:, 4 * n:4 * n + 4, :], h[:, 4 * n:4 * n + 4, :]).then_inc(out_done, 16)
            sp.wait_ge(out_done, 16 * 4)

        @block.gpsimd
        def _(pool):
            def add_square(n, c):
                pool.wait_ge(h_squared, C * n + c + 1)
                if c == 0:
                    nc.gpsimd.tensor_copy(hsum[:, :], sq[:, 0, :]).then_inc(h_added, 1)
                else:
                    pool.wait_ge(h_added, C * n + c)
                    nc.gpsimd.tensor_tensor(hsum[:, :], hsum[:, :], sq[:, c % BANKS, :], ALU.add).then_inc(h_added, 1)

            for c in range(C):
                add_square(0, c)
            for m, name in enumerate(MIXED):
                pool.wait_ge(rstd_ready, norm[name][1] + 1)
                y = y_ffn if name.startswith("ffn") else y_mix
                for c in range(DVE_SCALES, C + DVE_SCALES + POOL_LEAD):
                    if c < C:
                        nc.gpsimd.tensor_tensor(y[:, c, :], y[:, c, :], rstd_post[:, :], ALU.mult).then_inc(y_scaled, 1)
                    done = c - DVE_SCALES - POOL_LEAD
                    if m + 1 < len(SUMS) and done >= 0:
                        if done == 0:
                            pool.wait_ge(ss_ready, norm[SUMS[m]][1] + 1)
                        add_square(m + 1, done)

        @block.scalar
        def _(act):
            seen = Seen(act)
            split = [0]
            last_low = [None]
            warmed = [0]

            def split_hi(u0, j):
                slot = j % RING
                act.wait_ge(landed[slot], u0 * 4 + 16 * (j // RING + 1))
                if not isinstance(u0, int) or u0 + j >= RING:
                    act.wait_ge(units_used, u0 + (j + 1 - RING))
                nc.scalar.activation(w_hi[:, slot, :], raw[:, slot, :], ACT.Copy).then_inc(hi_ready, 1)

            def split_until(n):
                while split[0] < min(n, UNITS):
                    split_hi(split[0] // RING * RING, split[0] % RING)
                    split[0] += 1

            def load_table(func):
                n = warmed[0]
                warmed[0] += 1
                nc.scalar.activation(warm[0:1, n:n + 1], ones[0:1, 0:1], func)

            def low_free():
                if last_low[0] is not None:
                    read_out(act, last_low[0])

            def low_out(name, n=BANKS):
                filled(act, name)
                low_free()
                last_low[0] = name
                nc.scalar.activation(low[:, 0:n, :], banks(name)[:, 0:n, T:2 * T], ACT.Copy).then_inc(low_ready, 1)

            def root(name):
                which, n = norm[name]
                act.wait_ge(ss_ready, n + 1)
                if n:
                    act.wait_ge(rstd_ready, n)
                cols = slice(0 if name in ROW_SUMS else T, T + HALVES if name in TOKEN_SUMS else T)
                nc.scalar.activation(std[:, cols], bank_set(which)[:, BANKS - 1, cols], ACT.Sqrt,
                                     scale=1.0 / D, bias=const("eps")).then_inc(std_ready, 1)

            def output_group(y, name, group, g, gain=None):
                split_until(end[group] + (AHEAD if g < OUT_GROUPS - 1 else 2))
                scale = lambda b: 1.0 if gain is None else vec[:, gain, BANKS * g + b:BANKS * g + b + 1]
                m = MIXED.index(name)

                def square_group():
                    if g > 1:
                        act.wait_ge(y_added, m * Y_ADDED + g - 1)
                    nc.scalar.activation(sq[:, :, :], y[:, BANKS * (g - 1):BANKS * g, :], ACT.Square).then_inc(y_squared, 1)

                if g < OUT_GROUPS - 1:
                    if gain is None:
                        low_out(group)
                    else:
                        filled(act, group)
                        low_free()
                        last_low[0] = group
                        for b in range(BANKS):
                            ins = nc.scalar.activation(low[:, b, :], banks(group)[:, b, T:2 * T], ACT.Copy, scale=scale(b))
                        ins.then_inc(low_ready, 1)
                    if g:
                        square_group()
                    else:
                        load_table(ACT.Sqrt)
                    return
                low_free()
                last_low[0] = group
                for b in range(BANKS):
                    if b < BANKS - 1:
                        seen.next(bank_filled)
                    else:
                        filled(act, group)
                    nc.scalar.activation(low[:, b, :], banks(group)[:, b, T:2 * T], ACT.Copy, scale=scale(b)).then_inc(low_ready, 1)
                    if b == 0:
                        square_group()
                    if b == 1:
                        act.wait_ge(y_added, m * Y_ADDED + OUT_GROUPS - 1)
                    for done in ([], [0], [1, 2], [3])[b]:
                        if done < BANKS - 1:
                            act.wait_ge(y_ready, m * (BANKS - 1) + done + 1)
                        else:
                            read_out(act, group)
                        nc.scalar.activation(sq[:, done, :], y[:, BANKS * g + done, :], ACT.Square).then_inc(y_squared, 1)

            def square_h(src, name, c):
                if c >= BANKS:
                    act.wait_ge(h_added, C * SUMS.index(name) + c - BANKS + 1)
                nc.scalar.activation(sq[:, c % BANKS, :], src, ACT.Square).then_inc(h_squared, 1)

            def residual(gain, name, lag=LAG + 1, until=UNITS):
                for c in range(C):
                    seen.next(h_ready)
                    nc.scalar.activation(X[:, c, 0:T], h[:, c, :], ACT.Copy,
                                         scale=vec[:, gain, c:c + 1]).then_inc(x_hi_ready, 1)
                    square_h(h[:, c, :], name, c)
                    if c % 2 and c // 2 >= lag:
                        split_until(min(split[0] + 1, until))

            act.dma_start(vec[:, :, :], vectors).then_inc(consts_in, 16)
            act.dma_start(consts[:, :], constants).then_inc(consts_in, 16)
            act.dma_start(pos_i[:, :], positions.to_broadcast([ROT, T])).then_inc(pos_in, 16)
            act.wait_ge(consts_in, 32)
            for c in range(C):
                if c % 2 == 0:
                    act.wait_ge(mem_in[c // 2], 16)
                nc.scalar.activation(XM[:, c, 0:T], mem[:, c, :], ACT.Copy,
                                     scale=vec[:, MEM_GAIN, c:c + 1]).then_inc(x_hi_ready, 1)
                square_h(mem[:, c, :], "mem", c)
                if c % 2:
                    split_until(c // 2 + 1 if c // 2 < AHEAD else split[0] + 1)
                if c == 1:
                    for th in range(HALVES):
                        act.dma_start(x_tok[:, th, :], x_tokens[:, th, :]).then_inc(x_tok_in[th], 16)
                    act.dma_start(average[:, :, :], averages).then_inc(average_in, 16)
            act.dma_start(h[:, :, :], xT).then_inc(x_in, 16)
            load_table(ACT.Sqrt)
            act.wait_ge(x_squared, HALVES)
            nc.scalar.activation(x_rstd[:, 1, :], x_rstd[:, 0, :], ACT.Sqrt, scale=1.0 / D, bias=const("eps")).then_inc(x_std_ready, 1)

            def means_out(n):
                filled(act, ("means", n))
                for c in range(8 * n, 8 * n + 8):
                    nc.scalar.activation(X[:, c, 0:T], means_at(c), ACT.Copy, scale=vec[:, 0, c:c + 1]).then_inc(x_hi_ready, 1)

            split_until(end["mem_keys", 0] + AHEAD)
            root("mem")
            low_out(("mem_keys", 0))
            means_out(0)

            def memory_values(l):
                filled(act, ("mem_values", l))
                act.wait_ge(rstd_ready, 1)
                for th in range(HALVES):
                    ins = nc.scalar.activation((kv, kv1)[l][:, 1, 2 * th:2 * th + 2, :],
                                               banks(("mem_values", l))[:, th, :].rearrange("p (a t) -> p a t", a=2),
                                               ACT.Copy, scale=rstd_mem[:, T + th:T + th + 1])
                ins.then_inc(read_signal(("mem_values", l)), 1)

            split_until(end["mem_values", 0] + AHEAD)
            memory_values(0)
            means_out(1)
            act.wait_ge(ang_ready, 1)
            for n, table in enumerate((cos, sin)):
                nc.scalar.activation(table[:, :], red[:, n, :], ACT.Sin).then_inc(rope_ready, 1)
            for g in range(OUT_GROUPS):
                output_group(y_mix, "mixed0", ("pool", g), g, POOL_SCALE)
            split_until(start["mem_values", 1] + 6)
            root("mixed0")
            residual(2, "before_cross0", 0)
            memory_values(1)

            def cross_attention(l):
                split_until(end["cross_q", l] + AHEAD)
                root(f"before_cross{l}")
                load_table(ACT.Exp)
                low_out(("cross_q", l))
                name = ("cross", l)

                def head_T_out(hd):
                    act.wait_ge(head_filled, l * len(CROSS) + CROSS.index(("T", hd)) + 1)
                    nc.scalar.activation(xpT[:, hd, :, :], banks(name)[:, hd, :].rearrange("p (m t) -> p m t", m=2),
                                         ACT.Copy).then_inc(head_T, 1)

                def head_out(hd):
                    act.wait_ge(head_filled, l * len(CROSS) + CROSS.index(("o", hd)) + 1)
                    nc.scalar.activation(X[:, hd, 0:T], banks(name)[:, hd, 0:T], ACT.Copy).then_inc(att_hi_ready, 1)

                for hd in range(X_HEADS):
                    seen.next(npeak_ready)
                    for th in range(HALVES):
                        i = HALVES * hd + th
                        ins = nc.scalar.activation(xp[:, hd, th, :], banks(name)[:, hd, th * T:(th + 1) * T], ACT.Exp,
                                                   scale=cross_scale[:, 0, th:th + 1], bias=npeak[:, i:i + 1],
                                                   accum_out=total[:, i:i + 1])
                    ins.then_inc(exp_ready, 1)
                if l == 0:
                    split_until(start["mem_keys", 1] + 7)
                for hd in range(X_HEADS):
                    head_T_out(hd)
                if l == 0:
                    split_until(end["mem_keys", 1] + 2)
                for hd in range(X_HEADS):
                    head_out(hd)
                if l == 0:
                    split_until(end["mem_keys", 1] + AHEAD)
                    low_out(("mem_keys", 1))
                for g in range(OUT_GROUPS):
                    output_group(y_mix, f"crossed{l}", ("cross_out", l, g), g)
                root(f"crossed{l}")
                split_until(end["cross_out", l, OUT_GROUPS - 1] + AHEAD)
                residual(6 * l + 4, f"before_ffn{l}")

            def ffn(l):
                def glu(i, g):
                    which, n = place_of["glu", l, g]
                    before, m = place_of["glu", l, g - 1] if g else place_of["cross_out", l, OUT_GROUPS - 1]
                    act.wait_ge(units_used, i * (2 * FULL) + end["glu", l, g])
                    act.wait_ge(set_read[before], i + (m + 1))
                    nc.scalar.activation(low[:, :, :], bank_set(which)[:, :, T:2 * T], ACT.Copy).then_inc(low_ready, 1)
                    act.wait_ge(gu_scaled, i * 2 + (l * GLU_GROUPS + g + 1))
                    nc.scalar.activation(act_gate[:, :, :], gu[:, 0:2, :], ACT.Silu).then_inc(silu_ready, 1)
                    act.wait_ge(hid_ready, i * 2 + (l * GLU_GROUPS + g + 1))
                    nc.scalar.activation(hidden[:, bass.ds(i * 4 + 2 * g, 2), 0:T], hid[:, :, :], ACT.Copy).then_inc(hid_hi_ready, 1)

                for g in range(2):
                    split_until(end["glu", l, g] + AHEAD)
                    if g == 0:
                        root(f"before_ffn{l}")
                        load_table(ACT.Silu)
                    glu(0, g)
                with act.Fori(0, GLU_GROUPS // 2 - 1) as i:
                    for k in range(2):
                        for j in range(FULL):
                            split_hi(i * (2 * FULL) + split[0], FULL * k + j)
                        glu(i, 2 + k)
                split[0] += (GLU_GROUPS - 2) * FULL
                last_low[0] = "glu", l, GLU_GROUPS - 1
                for g in range(OUT_GROUPS):
                    if g == OUT_GROUPS - 1:
                        seen.count["bank_filled"] = seen.count.get("bank_filled", 0) + BANKS - 1
                    output_group(y_ffn, f"ffn{l}", ("down", l, g), g)
                root(f"ffn{l}")
                split_until(end["down", l, OUT_GROUPS - 1] + AHEAD)

            cross_attention(0)
            act.wait_ge(mem_keys_out, 2)
            read_out(act, ("mem_values", 1))
            act.dma_start(kv_store, kv1[:, :, :, :]).then_inc(kv_stored, 16)
            act.wait_ge(kv_stored, 16)
            ffn(0)
            residual(6, "before_mix1", until=end["idx"])

            act.dma_start(kv[:, :, :, :], kv_store).then_inc(kv_loaded, 16)
            split_until(end["idx"] + AHEAD)
            root("before_mix1")
            low_out("idx", 1)

            def sparse_turn(name):
                what, g = name
                if what == "logits":
                    filled(act, name)
                    if g:
                        act.wait_ge(scores_added, g)
                    nc.scalar.activation(masked[:, :, :], banks(name)[:, :, 0:KEYS], ACT.Relu, scale=SCALE).then_inc(read_signal(name), 1)
                elif what == "scores":
                    seen.next(npeak_ready)
                    for i in range(HALVES * BANKS):
                        b, th = divmod(i, HALVES)
                        cols = slice(0, P) if th == 0 else slice(P, KEYS)
                        ins = nc.scalar.activation(probs[:, b, cols], masked[:, b, cols], ACT.Exp,
                                                   scale=SCALE, bias=npeak[:, i:i + 1], accum_out=total[:, i:i + 1])
                        if i % BANKS == BANKS - 1:
                            ins.then_inc(exp_ready, 1)
                elif what == "T":
                    filled(act, name)
                    nc.scalar.activation(probsT[:, :, :], banks(name)[:, :, 0:KEYS], ACT.Copy).then_inc(read_signal(name), 1)
                else:
                    filled(act, name)
                    nc.scalar.activation(attended[:, BANKS * g:BANKS * g + BANKS, 0:T], banks(name)[:, :, 0:T], ACT.Copy).then_inc(att_hi_ready, 1)

            for name in SPARSE:
                for unit, turn in BESIDE.get(name, ()):
                    split_until(start[name] + unit + AHEAD)
                    sparse_turn(turn)
                if name == "values":
                    load_table(ACT.Exp)
                    split_until(end["values"] + AHEAD)
                    filled(act, "values")
                    act.wait_ge(rstd_ready, norm["before_mix1"][1] + 1)
                    for th in range(HALVES):
                        ins = nc.scalar.activation(values[:, th, :], banks("values")[:, th, :], ACT.Copy,
                                                   scale=rstd_pre[:, T + th:T + th + 1])
                    ins.then_inc(read_signal("values"), 1)
                elif name != ("att_out", 0):
                    split_until(end[name] + AHEAD)
                    low_out(name)
            for g in range(OUT_GROUPS):
                output_group(y_mix, "mixed1", ("att_out", g), g)
            root("mixed1")
            split_until(end["att_out", OUT_GROUPS - 1] + AHEAD)
            residual(6 + 2, "before_cross1")
            cross_attention(1)
            ffn(1)

        @block.vector
        def _(dve):
            seen = Seen(dve)
            split = [0]
            v = nc.vector

            def step(ins):
                ins.then_inc(dve_step, 1)
                seen.next(dve_step)

            def split_lo(u0, j):
                slot = j % RING
                dve.wait_ge(hi_ready, u0 + (j + 1))
                v.tensor_tensor(w_lo[:, slot, :], raw[:, slot, :], w_hi[:, slot, :].bitcast(F32), ALU.subtract).then_inc(lo_ready, 1)

            def split_until(n):
                while split[0] < min(n, UNITS):
                    split_lo(split[0] // RING * RING, split[0] % RING)
                    split[0] += 1

            def add_low(out, name, n=BANKS):
                seen.next(low_ready)
                v.tensor_tensor(out, banks(name)[:, 0:n, 0:T], low[:, 0:n, :], ALU.add).then_inc(read_signal(name), 1)
                read_out(dve, name)

            def one_over_root(name, out):
                n = norm[name][1]
                cols = slice(0 if name in ROW_SUMS else T, T + HALVES if name in TOKEN_SUMS else T)
                dve.wait_ge(std_ready, n + 1)
                v.reciprocal(out[:, cols], std[:, cols]).then_inc(rstd_ready, 1)
                dve.wait_ge(rstd_ready, n + 1)

            def x_low(src, gain, c, out, wait=1, signal=x_ready):
                if wait:
                    seen.next(x_hi_ready, wait)
                v.scalar_tensor_tensor(out[:, c, T:2 * T], src, vec[:, gain, c:c + 1],
                                       out[:, c, 0:T].bitcast(F32), ALU.mult, ALU.subtract).then_inc(signal, 1)

            def output_group(y, name, group, g, gain=None):
                split_until(end[group] + (AHEAD if g < OUT_GROUPS - 1 else 2))
                per_bank = g == OUT_GROUPS - 1
                out = banks(group)

                def add_bank(b):
                    c = BANKS * g + b
                    if gain is None:
                        return v.tensor_tensor(y[:, c, :], out[:, b, 0:T], low[:, b, :], ALU.add)
                    return v.scalar_tensor_tensor(y[:, c, :], out[:, b, 0:T], vec[:, gain, c:c + 1], low[:, b, :], ALU.mult, ALU.add)

                def add_squares():
                    seen.next(y_squared)
                    if g == 1:
                        v.tensor_copy(squares[:, :, :], sq[:, :, :]).then_inc(y_added, 1)
                    else:
                        v.tensor_tensor(squares[:, :, :], squares[:, :, :], sq[:, :, :], ALU.add).then_inc(y_added, 1)
                    seen.next(y_added)

                if not per_bank:
                    if gain is None:
                        add_low(y[:, BANKS * g:BANKS * g + BANKS, :], group)
                    else:
                        seen.next(low_ready)
                        for b in range(BANKS):
                            ins = add_bank(b)
                        ins.then_inc(read_signal(group), 1)
                        read_out(dve, group)
                    if g:
                        add_squares()
                    return
                for b in range(BANKS):
                    seen.next(low_ready)
                    add_bank(b).then_inc(y_ready if b < BANKS - 1 else read_signal(group), 1)
                    if b == 0:
                        add_squares()
                    if b == BANKS - 2:
                        step(v.tensor_tensor(squares[:, 0:2, :], squares[:, 0:2, :], squares[:, 2:4, :], ALU.add))
                        v.tensor_tensor(squares[:, 0, :], squares[:, 0, :], squares[:, 1, :], ALU.add).then_inc(y_added, 1)
                        seen.next(y_added)
                seen.next(y_ready, BANKS - 1)
                read_out(dve, group)
                seen.next(y_squared, BANKS)

            def residual(y, name, gain, next_gain=None, lag=LAG, until=UNITS):
                one_over_root(name, rstd_post)
                done = MIXED.index(name) * C
                for c in range(C):
                    if c < DVE_SCALES:
                        step(v.tensor_tensor(y[:, c, :], y[:, c, :], rstd_post[:, :], ALU.mult))
                    else:
                        seen.next(y_scaled)
                    v.scalar_tensor_tensor(h[:, c, :], y[:, c, :], vec[:, gain, c:c + 1], h[:, c, :],
                                           ALU.mult, ALU.add).then_inc(h_ready, 1)
                    if next_gain is None:
                        continue
                    if c:
                        dve.wait_ge(h_ready, done + c)
                        x_low(h[:, c - 1, :], next_gain, c - 1, X)
                    if c == C - 1:
                        dve.wait_ge(h_ready, done + C)
                        x_low(h[:, c, :], next_gain, c, X)
                    if c % 2 and c // 2 >= lag:
                        split_until(min(split[0] + 1, until))

            def rotate(q, n):
                src, dst = q[0:ROT], swap[:, 0:n, :]
                step(v.stream_shuffle(dst, src, [(r + ROT // 2) % ROT for r in range(ROT)]))
                step(v.tensor_tensor(dst, dst, over(sin[:, :], n), ALU.mult))
                step(v.tensor_tensor(src, src, over(cos[:, :], n), ALU.mult))
                v.tensor_tensor(src, src, dst, ALU.add).then_inc(q_ready, 1)
                seen.next(q_ready)

            dve.wait_ge(consts_in, 32)
            for c in range(C):
                if c % 2 == 0:
                    dve.wait_ge(mem_in[c // 2], 16)
                x_low(mem[:, c, :], MEM_GAIN, c, XM)
                if c % 2:
                    split_until(c // 2 + 1 if c // 2 < AHEAD else split[0] + 1)
            for th in range(HALVES):
                dve.wait_ge(x_tok_in[th], 16)
                v.tensor_tensor_reduce(x_square[:, th, :], x_tok[:, th, :], x_tok[:, th, :], 1.0, 0.0,
                                       ALU.mult, ALU.add, x_rstd[:, 0, th:th + 1]).then_inc(x_squared, 1)
            dve.wait_ge(x_std_ready, 1)
            step(v.reciprocal(x_rstd[:, 2, :], x_rstd[:, 1, :]))
            for th in range(HALVES):
                v.tensor_scalar(x_tok[:, th, :], x_tok[:, th, :], x_rstd[:, 2, th:th + 1], None, ALU.mult).then_inc(x_normed, 1)
            def rotary_angles():
                dve.wait_ge(pos_in, 16)
                step(v.tensor_copy(pos_f[:, :], pos_i[:, :]))
                step(v.tensor_scalar(ang[:, :], pos_f[:, :], const("inv")[0:ROT, :], None, ALU.mult))
                for n, quarter in enumerate((0.25, 0.0)):
                    r = red[:, n, :]
                    step(v.tensor_scalar(turns_[:, :], ang[:, :], float(1 / (2 * np.pi)), quarter, ALU.mult, ALU.add))
                    step(v.tensor_scalar(turns_[:, :], turns_[:, :], ROUND, None, ALU.add))
                    step(v.tensor_scalar(turns_[:, :], turns_[:, :], -ROUND, None, ALU.add))
                    step(v.scalar_tensor_tensor(r, turns_[:, :], -TWO_PI_A, ang[:, :], ALU.mult, ALU.add))
                    step(v.scalar_tensor_tensor(r, turns_[:, :], -TWO_PI_B, r, ALU.mult, ALU.add))
                    step(v.scalar_tensor_tensor(r, turns_[:, :], -TWO_PI_C, r, ALU.mult, ALU.add))
                    if quarter:
                        step(v.tensor_scalar(r, r, float(np.pi / 2), PI_BELOW, ALU.add, ALU.min))
                    else:
                        step(v.tensor_scalar(r, r, PI_BELOW, None, ALU.min))
                    step(v.tensor_scalar(r, r, -PI_BELOW, None, ALU.max))
                v.tensor_scalar(red[:, 1, :], red[:, 1, :], const("sign")[0:ROT, :], None, ALU.mult).then_inc(ang_ready, 1)

            def memory_keys(l):
                keys_out = (kv, kv1)[l][:, 0, :, :]
                add_low(keys_out, ("mem_keys", l))
                v.tensor_tensor(keys_out, keys_out, over(rstd_mem[:, 0:T], BANKS), ALU.mult).then_inc(mem_keys_out, 1)

            def means_out(n):
                for c in range(8 * n, 8 * n + 8):
                    x_low(means_at(c), 0, c, X, 2 - c % 2 * 2, read_signal(("means", n)) if c % 8 == 7 else x_ready)

            split_until(end["mem_keys", 0] + AHEAD)
            one_over_root("mem", rstd_mem)
            memory_keys(0)
            means_out(0)
            split_until(start["mem_values", 0] + 7)
            rotary_angles()
            split_until(end["mem_values", 0] + AHEAD)
            means_out(1)
            dve.wait_ge(x_in, 16)
            for g in range(OUT_GROUPS):
                output_group(y_mix, "mixed0", ("pool", g), g, POOL_SCALE)
            split_until(start["mem_values", 1] + 6)
            residual(y_mix, "mixed0", 1, 2, 1)

            def normalise(p, i, n, signal):
                step(v.reciprocal(rtotal[:, i:i + n], total[:, i:i + n]))
                for i in range(i, i + n):
                    ins = v.tensor_scalar(p(i), p(i), rtotal[:, i:i + 1], None, ALU.mult)
                ins.then_inc(signal, 1)
                seen.next(signal)

            def cross_attention(l):
                split_until(end["cross_q", l] + AHEAD)
                one_over_root(f"before_cross{l}", rstd_pre)
                step(v.tensor_scalar(cross_scale[:, 0, :], rstd_pre[:, T:T + HALVES], SCALE, None, ALU.mult))
                step(v.tensor_scalar(cross_scale[:, 1, :], rstd_pre[:, T:T + HALVES], -SCALE, None, ALU.mult))
                seen.next(low_ready)
                name = "cross_q", l
                v.tensor_tensor(xq[:, :, :], banks(name)[:, :, 0:T], low[:, :, :], ALU.add).then_inc(read_signal(name), 1)
                name = "cross", l

                def order(what, hd):
                    return l * len(CROSS) + CROSS.index((what, hd)) + 1

                def head_peak(hd):
                    i = HALVES * hd
                    dve.wait_ge(head_filled, order("s", hd))
                    step(v.reduce_max(peak[:, i:i + HALVES], banks(name)[:, hd, :].rearrange("p (t m) -> p t m", t=HALVES), AX_X))
                    v.tensor_tensor(npeak[:, i:i + HALVES], peak[:, i:i + HALVES], cross_scale[:, 1, :], ALU.mult).then_inc(npeak_ready, 1)

                def head_probs(hd):
                    seen.next(exp_ready)
                    normalise(lambda i: xp[:, i // HALVES, i % HALVES, :], HALVES * hd, HALVES, probs_ready)

                for hd in range(X_HEADS):
                    head_peak(hd)
                    if hd:
                        head_probs(hd - 1)
                head_probs(X_HEADS - 1)
                if l == 0:
                    split_until(end["mem_keys", 1] + 2)
                for hd in range(X_HEADS):
                    seen.next(att_hi_ready)
                    v.tensor_tensor(X[:, hd, T:2 * T], banks(name)[:, hd, 0:T], X[:, hd, 0:T].bitcast(F32),
                                    ALU.subtract).then_inc(att_ready if hd < X_HEADS - 1 else read_signal(name), 1)
                if l == 0:
                    split_until(end["mem_keys", 1] + AHEAD)
                    memory_keys(1)
                for g in range(OUT_GROUPS):
                    output_group(y_mix, f"crossed{l}", ("cross_out", l, g), g)
                residual(y_mix, f"crossed{l}", 6 * l + 3, 6 * l + 4)

            def ffn(l):
                low_before = seen.count["low_ready"]

                def glu(i, g):
                    which, n = place_of["glu", l, g]
                    out = bank_set(which)
                    dve.wait_ge(low_ready, i * 2 + (low_before + g + 1))
                    if l or g:
                        dve.wait_ge(hidden_ready, i * 2 + (l * GLU_GROUPS + g))
                    v.tensor_tensor(gu[:, :, :], out[:, :, 0:T], low[:, :, :], ALU.add).then_inc(set_read[which], 1)
                    dve.wait_ge(set_read[which], i + (n + 1))
                    v.tensor_tensor(gu[:, :, :], gu[:, :, :], over(rstd_pre[:, 0:T], BANKS), ALU.mult).then_inc(gu_scaled, 1)
                    dve.wait_ge(gu_scaled, i * 2 + (l * GLU_GROUPS + g + 1))
                    dve.wait_ge(silu_ready, i * 2 + (l * GLU_GROUPS + g + 1))
                    v.tensor_tensor(hid[:, :, :], act_gate[:, :, :], gu[:, 2:4, :], ALU.mult).then_inc(hid_ready, 1)
                    dve.wait_ge(hid_ready, i * 2 + (l * GLU_GROUPS + g + 1))
                    dve.wait_ge(hid_hi_ready, i * 2 + (l * GLU_GROUPS + g + 1))
                    v.tensor_tensor(hidden[:, bass.ds(i * 4 + 2 * g, 2), T:2 * T], hid[:, :, :],
                                    hidden[:, bass.ds(i * 4 + 2 * g, 2), 0:T].bitcast(F32), ALU.subtract).then_inc(hidden_ready, 1)

                for g in range(2):
                    split_until(end["glu", l, g] + AHEAD)
                    if g == 0:
                        one_over_root(f"before_ffn{l}", rstd_pre)
                    glu(0, g)
                with dve.Fori(0, GLU_GROUPS // 2 - 1) as i:
                    for k in range(2):
                        for j in range(FULL):
                            split_lo(i * (2 * FULL) + split[0], FULL * k + j)
                        glu(i, 2 + k)
                split[0] += (GLU_GROUPS - 2) * FULL
                seen.count["low_ready"] += GLU_GROUPS
                dve.wait_ge(hidden_ready, (l + 1) * GLU_GROUPS)
                for g in range(OUT_GROUPS):
                    output_group(y_ffn, f"ffn{l}", ("down", l, g), g)

            cross_attention(0)
            ffn(0)
            residual(y_ffn, "ffn0", 5, 6, until=end["idx"])

            split_until(end["idx"] + AHEAD)
            one_over_root("before_mix1", rstd_pre)
            filled(dve, "idx")
            for th in range(HALVES):
                step(v.tensor_scalar(iw[:, th, :], banks("idx")[:, 1 + th, 0:IDX_HEADS], rstd_pre[:, T + th:T + th + 1], IW_SCALE,
                                     ALU.mult, ALU.mult))
            add_low(ik[:, :].unsqueeze(1), "idx", 1)
            step(v.tensor_tensor(ik[:, :], ik[:, :], rstd_pre[:, 0:T], ALU.mult))
            rotate(ik[:, :].unsqueeze(1), 1)

            def heads_out(q, name):
                split_until(end[name] + AHEAD)
                add_low(q[:, :, :], name)
                step(v.tensor_tensor(q[:, :, :], q[:, :, :], over(rstd_pre[:, 0:T], BANKS), ALU.mult))
                rotate(q, BANKS)

            def take_8():
                for th, cols in enumerate((slice(0, P), slice(P, KEYS))):
                    step(v.max(top8[:, th, :], work[:, cols]))
                    step(v.match_replace(work[:, cols], top8[:, th, :], work[:, cols], TAKEN))

            def sparse_turn(name):
                what, g = name
                if what == "logits":
                    read_out(dve, name)
                    for b in range(BANKS):
                        for th, cols in enumerate((slice(0, P), slice(P, KEYS))):
                            hd = BANKS * g + b
                            ins = v.scalar_tensor_tensor(score[:, cols], masked[:, b, cols], iw[:, th, hd:hd + 1], score[:, cols],
                                                         ALU.mult, ALU.add)
                            if th == 1 and b == BANKS - 1:
                                ins.then_inc(scores_added, 1)
                                seen.next(scores_added)
                            else:
                                step(ins)
                elif what == "scores":
                    filled(dve, name)
                    for i in range(HALVES * BANKS):
                        b, th = divmod(i, HALVES)
                        cols = slice(0, P) if th == 0 else slice(P, KEYS)
                        ins = v.tensor_tensor_reduce(masked[:, b, cols], banks(name)[:, b, cols], mask[:, cols], 1.0, TAKEN,
                                                     ALU.add, ALU.max, peak[:, i:i + 1])
                    ins.then_inc(read_signal(name), 1)
                    read_out(dve, name)
                    v.tensor_scalar(npeak[:, :], peak[:, :], -SCALE, None, ALU.mult).then_inc(npeak_ready, 1)
                    for half in range(2):
                        seen.next(exp_ready)
                        normalise(lambda i: probs[:, i // HALVES, slice(0, P) if i % HALVES == 0 else slice(P, KEYS)],
                                  half * BANKS, BANKS, probs_ready)
                elif what == "o":
                    seen.next(att_hi_ready)
                    out = attended[:, BANKS * g:BANKS * g + BANKS]
                    v.tensor_tensor(out[:, :, T:2 * T], banks(name)[:, :, 0:T], out[:, :, 0:T].bitcast(F32),
                                    ALU.subtract).then_inc(read_signal(name), 1)

            step(v.memset(score[:, :], 0.0))
            for name in SPARSE:
                for unit, turn in BESIDE.get(name, ()):
                    split_until(start[name] + unit + AHEAD)
                    sparse_turn(turn)
                if name == "values":
                    step(v.tensor_tensor(work[:, :], score[:, :], causal, ALU.add))
                    for _ in range(TOPK // 8):
                        split_until(split[0] + 1)
                        take_8()
                    step(v.tensor_scalar(mask[:, :], work[:, :], TAKEN_BELOW, NEG, ALU.is_gt, ALU.mult))
                    step(v.tensor_tensor(mask[:, :], mask[:, :], causal, ALU.add))
                elif name == "keys":
                    heads_out(keys, name)
                elif name[0] in ("iq", "q"):
                    heads_out(quad[name[1] % 2], name)
            for g in range(OUT_GROUPS):
                output_group(y_mix, "mixed1", ("att_out", g), g)
            residual(y_mix, "mixed1", 6 + 1, 6 + 2)
            cross_attention(1)
            ffn(1)
            residual(y_ffn, "ffn1", 6 + 5)

        @block.tensor
        def _(pe):
            seen = Seen(pe)
            mm = nc.tensor.matmul

            def set_free(name, i=0):
                which, n = place_of[name]
                if n:
                    pe.wait_ge(set_read[which], i + n)

            def sum_squares(name):
                which, n = norm[name]
                out = bank_set(which)[:, BANKS - 1, :]
                if plan.set_before[name]:
                    pe.wait_ge(set_read[which], plan.set_before[name])
                if name in MIXED:
                    m = MIXED.index(name)
                    for b in range(BANKS):
                        if b == BANKS - 1:
                            pe.wait_ge(y_added, (m + 1) * Y_ADDED)
                            mm(out[:, 0:T], ones, squares[:, 0, :], start=False, stop=False)
                        pe.wait_ge(y_squared, m * Y_SQUARED + OUT_GROUPS + b)
                        ins = mm(out[:, 0:T], ones, sq[:, b, :], start=b == 0, stop=b == BANKS - 1)
                else:
                    pe.wait_ge(h_added, (SUMS.index(name) + 1) * C)
                    if name in ROW_SUMS:
                        ins = mm(out[:, 0:T], ones, hsum[:, :], start=True, stop=True)
                if name in TOKEN_SUMS:
                    for th in range(HALVES):
                        ins = mm(out[:, T + th:T + th + 1], hsum[:, th * P:th * P + P], ones[:, 0:1], start=True, stop=True)
                ins.then_inc(ss_ready, 1)

            def group(name, units, x, x_wait=None, i=0, unit_step=0, between={}, bank_by_bank=False):
                set_free(name, i)
                out, u0 = banks(name), start[name]

                def product(j, kk, b):
                    k, slot = 2 * j + kk, (u0 + j) % RING
                    if k == 0 and b == BANKS - 1 and name in plan.sum_before:
                        pe.wait_ge(std_ready, norm[plan.sum_before[name]][1] + 1)
                    w = slice(kk * BANKS * P + b * P, kk * BANKS * P + b * P + P)
                    mm(out[:, b, :], w_hi[:, slot, w], x(k), start=k == 0, stop=False)
                    return mm(out[:, b, T:2 * T], w_lo[:, slot, w], x(k)[:, 0:T], start=False, stop=k == 2 * units - 1)

                def arrived(j):
                    pe.wait_ge(lo_ready, (i * unit_step if unit_step else 0) + (u0 + j + 1))

                for j in range(units - 2 if bank_by_bank else units):
                    if j in between:
                        between[j]()
                    arrived(j)
                    for kk in range(2):
                        if x_wait:
                            x_wait(2 * j + kk)
                        for b in range(BANKS):
                            ins = product(j, kk, b)
                    ins.then_inc(units_used, 1)
                if bank_by_bank:
                    for b in range(BANKS):
                        for j in range(units - 2, units):
                            if b == 0:
                                arrived(j)
                            for kk in range(2):
                                if b == 0 and x_wait:
                                    x_wait(2 * j + kk)
                                ins = product(j, kk, b)
                        if b < BANKS - 1:
                            ins.then_inc(bank_filled, 1)
                    ins.then_inc(units_used, 2)

            def named(name, x, x_wait=None, **more):
                group(name, end[name] - start[name], x, x_wait, **more)

            def tokens_product(out, x, w_h, w_l, first, last):
                for th in range(HALVES):
                    o = out(th)
                    hi = x[:, th * P:th * P + P]
                    mm(o, hi, w_h, start=first, stop=False)
                    mm(o, hi, w_l, start=False, stop=False)
                    ins = mm(o, x[:, T + th * P:T + th * P + P], w_h, start=False, stop=last)
                return ins

            def token_group(name, x, between={}):
                set_free(name)
                for j in range(FULL):
                    if j in between:
                        between[j]()
                    u = start[name] + j
                    pe.wait_ge(lo_ready, u + 1)
                    for kk in range(2):
                        k = 2 * j + kk
                        w = slice(kk * BANKS * P, (kk + 1) * BANKS * P)
                        ins = tokens_product(lambda th: banks(name)[:, th, :], x(k), w_hi[:, u % RING, w], w_lo[:, u % RING, w],
                                             k == 0, k == C - 1)
                    ins.then_inc(units_used, 1)

            def in_X(k):
                return X[:, k, :]

            def in_XM(k):
                return XM[:, k, :]

            def in_attended(k):
                return attended[:, k, :]

            def next_x(k):
                seen.next(x_ready)

            def means(n):
                name = "means", n
                set_free(name)
                if n == 0:
                    pe.wait_ge(average_in, 16)
                    pe.wait_ge(x_normed, HALVES)
                for c in range(8 * n, 8 * n + 8):
                    if c == 8 * n + 6 and name in plan.sum_before:
                        pe.wait_ge(std_ready, norm[plan.sum_before[name]][1] + 1)
                    a, out = average[:, c // BANKS, :], means_at(c)
                    mm(out[:, 0:REACH], x_tok[:, 0, c * P:c * P + P], a[:, 0:REACH], start=True, stop=False, skip_group_check=True)
                    mm(out[:, P:REACH], x_tok[:, 1, c * P:c * P + P], a[:, REACH:REACH + REACH - P], start=False, stop=False, skip_group_check=True)
                    ins = mm(out[:, REACH:T], x_tok[:, 1, c * P:c * P + P], a[:, 2 * REACH - P:REACH + P], start=False, stop=True, skip_group_check=True)
                ins.then_inc(psum_filled, 1)

            pe.wait_ge(consts_in, 32)
            named(("mem_keys", 0), in_XM, next_x)
            sum_squares("mem")
            means(0)
            token_group(("mem_values", 0), in_XM)
            means(1)
            def mean_there(c):
                if c % 8 == 7:
                    read_out(pe, ("means", c // 8))
                else:
                    seen.next(x_ready)

            for g in range(OUT_GROUPS):
                named(("pool", g), lambda k: X[:, BANKS * g + k, :], lambda k: mean_there(BANKS * g + k),
                      bank_by_bank=g == OUT_GROUPS - 1)
            token_group(("mem_values", 1), in_XM, {2: lambda: sum_squares("mixed0")})

            def cross_attention(l):
                name = "cross", l
                out = banks(name)

                def scores():
                    set_free(name)
                    read_out(pe, ("cross_q", l))
                    if l:
                        pe.wait_ge(kv_loaded, 16)
                    else:
                        pe.wait_ge(mem_keys_out, 1)
                    for hd in range(X_HEADS):
                        for th in range(HALVES):
                            ins = mm(out[:, hd, th * T:th * T + T], xq[:, hd, th * P:th * P + P], kv[:, 0, hd, :], start=True, stop=True)
                        ins.then_inc(head_filled, 1)

                def transposed(hd):
                    pe.wait_ge(probs_ready, probs_before[l] + hd + 1)
                    for m in range(2):
                        for th in range(HALVES):
                            ins = nc.tensor.transpose(out[:, hd, m * T + th * P:m * T + th * P + P],
                                                      xp[:, hd, th, m * P:m * P + P], ident)
                    ins.then_inc(head_filled, 1)

                def output(hd):
                    pe.wait_ge(head_T, l * X_HEADS + hd + 1)
                    for m in range(2):
                        ins = mm(out[:, hd, 0:T], kv[:, 1, 2 * m + hd // 2, hd % 2 * P:hd % 2 * P + P], xpT[:, hd, m, :],
                                 start=m == 0, stop=m == 1)
                    ins.then_inc(head_filled, 1)

                named(("cross_q", l), in_X, next_x)
                sum_squares(f"before_cross{l}")
                if l == 0:
                    named(("mem_keys", 1), in_XM, between={
                        1: scores, 4: lambda: [transposed(hd) for hd in range(X_HEADS)],
                        6: lambda: [output(hd) for hd in range(X_HEADS)]})
                else:
                    scores()
                    for what, hd in CROSS[X_HEADS:]:
                        (transposed if what == "T" else output)(hd)

                def attention_there(k):
                    if k < X_HEADS - 1:
                        pe.wait_ge(att_ready, l * (X_HEADS - 1) + k + 1)
                    else:
                        read_out(pe, name)

                for g in range(OUT_GROUPS):
                    named(("cross_out", l, g), in_X, attention_there if g == 0 else None, bank_by_bank=g == OUT_GROUPS - 1)
                sum_squares(f"crossed{l}")

            def ffn(l):
                named(("glu", l, 0), in_X, next_x)
                sum_squares(f"before_ffn{l}")
                named(("glu", l, 1), in_X)
                with pe.Fori(0, GLU_GROUPS // 2 - 1) as i:
                    for k in range(2):
                        group(("glu", l, 2 + k), FULL, in_X, i=i, unit_step=2 * FULL)

                def hidden_there(k):
                    if k % 2 == 0:
                        pe.wait_ge(hidden_ready, l * GLU_GROUPS + k // 2 + 1)

                with pe.Fori(0, OUT_GROUPS // 2) as i:
                    for k in range(2):
                        group(("down", l, k), DOWN, lambda c: hidden[:, c, :], hidden_there if k == 0 else None,
                              i=i, unit_step=2 * DOWN, bank_by_bank=k == 1)
                sum_squares(f"ffn{l}")

            cross_attention(0)
            ffn(0)

            set_free("idx")
            out = banks("idx")
            for j in range(IDX_UNITS):
                u = start["idx"] + j
                pe.wait_ge(lo_ready, u + 1)
                for kk in range(4):
                    k = 4 * j + kk
                    seen.next(x_ready)
                    w = slice(kk * 2 * P, kk * 2 * P + P)
                    mm(out[:, 0, :], w_hi[:, u % RING, w], X[:, k, :], start=k == 0, stop=False)
                    mm(out[:, 0, T:2 * T], w_lo[:, u % RING, w], X[:, k, 0:T], start=False, stop=k == C - 1)
                    w = slice(kk * 2 * P + P, kk * 2 * P + P + IDX_HEADS)
                    ins = tokens_product(lambda th: out[:, 1 + th, 0:IDX_HEADS], X[:, k, :], w_hi[:, u % RING, w],
                                         w_lo[:, u % RING, w], k == 0, k == C - 1)
                ins.then_inc(units_used, 1)
            sum_squares("before_mix1")

            def query_key(name, q, k):
                set_free(name)
                seen.next(q_ready)
                for b in range(BANKS):
                    mm(banks(name)[:, b, 0:P], q[:, b, 0:P], k[:, 0:P], start=True, stop=True)
                    ins = mm(banks(name)[:, b, P:KEYS], q[:, b, P:T], k, start=True, stop=True)
                ins.then_inc(psum_filled, 1)

            def sparse_turn(name):
                what, g = name
                if what == "logits":
                    query_key(name, quad[g % 2], ik[:, :])
                elif what == "scores":
                    query_key(name, quad[g % 2], keys[:, g, :])
                elif what == "T":
                    set_free(name)
                    pe.wait_ge(probs_ready, probs_before[0] + X_HEADS + 2 * (g + 1))
                    for b in range(BANKS):
                        for n in range(KEYS // P):
                            ins = nc.tensor.transpose(banks(name)[:, b, n * P:n * P + P], probs[:, b, n * P:n * P + P], ident)
                    ins.then_inc(psum_filled, 1)
                else:
                    set_free(name)
                    read_out(pe, ("T", g))
                    if g == 0:
                        read_out(pe, "values")
                    for b in range(BANKS):
                        mm(banks(name)[:, b, 0:T], values[:, 0, g * P:g * P + P], probsT[:, b, 0:T], start=True, stop=False)
                        ins = mm(banks(name)[:, b, P:T], values[:, 1, g * P:g * P + P], probsT[:, b, T:KEYS], start=False, stop=True)
                    ins.then_inc(psum_filled, 1)

            for name in SPARSE:
                beside = {}
                for unit, turn in BESIDE.get(name, ()):
                    beside.setdefault(unit, []).append(turn)
                between = {unit: lambda turns=turns: [sparse_turn(turn) for turn in turns] for unit, turns in beside.items()}
                if name == ("iq", 1):
                    seen.next(q_ready)
                if name == ("q", 1):
                    seen.next(q_ready)
                if name == "values":
                    token_group(name, in_X, between)
                elif name[0] == "att_out":
                    named(name, in_attended, lambda k: read_out(pe, ("o", k // BANKS)) if k % BANKS == 0 else None, between=between)
                else:
                    named(name, in_X, between=between)
            for g in range(1, OUT_GROUPS):
                named(("att_out", g), in_attended, bank_by_bank=g == OUT_GROUPS - 1)
            sum_squares("mixed1")
            cross_attention(1)
            ffn(1)


def _units(w):
    k = w.shape[0] // (2 * P)
    return w.reshape(k, 2, P, BANKS * P).transpose(0, 2, 1, 3).reshape(k, P, UNIT)


def kernel(**inputs):
    import concourse.bacc as bacc
    from concourse.bass_utils import run_bass_kernel_spmd

    a = {k: np.asarray(v) for k, v in inputs.items()}
    w_in, w_out = a["dsa_w_in"][0], a["dsa_w_out"][0]
    edges = np.cumsum([0, HEADS * P, KV_HEADS * P, KV_HEADS * P, IDX_HEADS * P, P, IDX_HEADS])
    q, k, v, iq, ik, iw = (w_in[:, x:y] for x, y in zip(edges, edges[1:]))
    W = BANKS * P
    stream = np.empty((UNITS, P, UNIT), np.float32)
    plan = Plan()
    for name, n in plan.weights:
        at = plan.start[name]
        kind, l, g = (tuple(name) if isinstance(name, tuple) else (name,)) + (None,) * (3 - (len(name) if isinstance(name, tuple) else 1))
        cols = lambda w, g: w[:, g * W:(g + 1) * W]
        if kind == "idx":
            both = np.concatenate([ik, iw, np.zeros((D, 2 * P - P - IDX_HEADS), np.float32)], 1)
            stream[at:at + n] = both.reshape(n, 4, P, 2 * P).transpose(0, 2, 1, 3).reshape(n, P, UNIT)
            continue
        if kind == "mem_keys":
            w = cols(a["xattn_wkv"][l], 0)
        elif kind == "mem_values":
            w = cols(a["xattn_wkv"][l], 1)
        elif kind == "pool":
            w = a["pool_w"][0, l]
        elif kind == "cross_q":
            w = a["xattn_wq"][l]
        elif kind == "cross_out":
            w = cols(a["xattn_wo"][l], g)
        elif kind == "glu":
            gate = a["ffn_w_gate_up"][l][:, 2 * P * g:2 * P * (g + 1)]
            up = a["ffn_w_gate_up"][l][:, D_FF + 2 * P * g:D_FF + 2 * P * (g + 1)]
            w = np.concatenate([gate, up], 1)
        elif kind == "down":
            w = cols(a["ffn_w_down"][l], g)
        elif kind == "iq":
            w = cols(iq, l)
        elif kind == "q":
            w = cols(q, l)
        elif kind == "keys":
            w = k
        elif kind == "values":
            w = v
        else:
            w = cols(w_out, l)
        stream[at:at + n] = _units(w)

    def by_feature(x):
        return np.ascontiguousarray(x.T.reshape(C, P, x.shape[0]).transpose(1, 0, 2))

    gains = np.concatenate([a["norm_gains"].reshape(6 * LAYERS, D), a["mem_norm"][None], a["pool_scale"]])
    vectors = np.ascontiguousarray(gains.reshape(N_GAINS, C, P).transpose(2, 0, 1))
    consts = np.zeros((P, N_CONST), np.float32)
    put = lambda name, x: consts.__setitem__((slice(0, x.shape[0]), slice(CONST_AT[name], CONST_AT[name] + CONST[name])), x)
    put("ident", np.eye(P, dtype=np.float32))
    put("ones", np.ones((P, P), np.float32))
    query, key = np.arange(P)[:, None], np.arange(T)[None]
    put("causal", np.concatenate([np.where(key[:, :P] <= query, 0, NEG), np.where(key <= query + P, 0, NEG)], 1).astype(np.float32))
    t_in, t_out = np.arange(P)[:, None], np.arange(T)[None]
    averages = np.zeros((P, len(POOL_WINDOWS), REACH + P), np.float32)
    for n, w in enumerate(POOL_WINDOWS):
        for t_from, cols, at in ((0, slice(0, REACH), slice(0, REACH)), (P, slice(P, T), slice(REACH, REACH + P))):
            age = t_out - (t_in + t_from)
            mean = ((age >= 0) & (age < w)) / np.minimum(t_out + 1, w).astype(np.float32) - (age == 0)
            averages[:, n, at] = mean[:, cols]
    inv = np.float32(500000.0) ** (-np.arange(0, ROT, 2, dtype=np.float32) / np.float32(ROT))
    put("inv", np.concatenate([inv, inv])[:, None])
    put("sign", np.concatenate([-np.ones(ROT // 2), np.ones(ROT // 2)])[:, None].astype(np.float32))
    put("eps", np.full((P, 1), EPS, np.float32))
    arrays = {
        "xT": by_feature(a["x"][0]), "x_tokens": np.ascontiguousarray(a["x"][0].reshape(HALVES, P, D).transpose(1, 0, 2)),
        "memT": by_feature(a["mem"][0]), "positions": np.ascontiguousarray(a["positions"], np.int32), "averages": averages,
        "vectors": vectors, "constants": consts, "weights": stream,
    }
    nc = bacc.Bacc("TRN2", target_bir_lowering=False, num_devices=1)
    args = [nc.dram_tensor(n, x.shape, mybir.dt.from_np(x.dtype), kind="ExternalInput").ap() for n, x in arrays.items()]
    out = nc.dram_tensor("outT", (P, C, T), F32, kind="ExternalOutput").ap()
    kv_store = nc.dram_tensor("kv_store", (P, 2, BANKS, T), F32, kind="Internal").ap()
    hybrid_trunk(nc, *args, out, kv_store)
    result = run_bass_kernel_spmd(nc, [arrays], core_ids=[0])
    got = result.results[0]["outT"]
    return np.ascontiguousarray(got.transpose(2, 1, 0).reshape(1, T, D))
```

```python
import numpy as np
import concourse.bass as bass
from concourse import mybir
from contextlib import ExitStack

F32 = mybir.dt.float32
F32R = mybir.dt.float32r
I32 = mybir.dt.int32
ALU = mybir.AluOpType
ACT = mybir.ActivationFunctionType
AX_X = mybir.AxisListType.X

P = 128
T = 256
HALVES = T // P
D = 2048
C = D // P
D_FF = 5632
CF = D_FF // P
LAYERS = 2
POOL_WINDOWS = (2, 4, 8, 16)
REACH = P + max(POOL_WINDOWS)
HEADS, KV_HEADS, IDX_HEADS, X_HEADS = 16, 4, 16, 4
ROT = P // 4
TOPK = T // 4
EPS = 1e-6
SCALE = float(P) ** -0.5
IW_SCALE = float(IDX_HEADS) ** -0.5
NEG = -1e30
TAKEN = -3e38
TAKEN_BELOW = -2e38

UNIT = 1024
RING = 4
AHEAD = 4
LAG = 1
OUT_PARTS = (0, 4), (4, 8), (8, 12), (12, 14), (14, 16)
MEM_PARTS = C // 2
BANKS = 4
FULL = C // 2
PAIR = 2
DOWN = CF // 2
GLU_GROUPS = D_FF // (2 * P)
OUT_GROUPS = C // BANKS
IDX_UNITS = C // 4
UNITS = (4 * FULL + OUT_GROUPS * PAIR + LAYERS * (FULL + OUT_GROUPS * PAIR + GLU_GROUPS * FULL + OUT_GROUPS * DOWN)
         + IDX_UNITS + 10 * FULL + OUT_GROUPS * FULL)

N_GAINS = 6 * LAYERS + 2
MEM_GAIN, POOL_SCALE = 6 * LAYERS, 6 * LAYERS + 1
KEYS = P + T
CONST = {"ident": P, "ones": P, "causal": KEYS, "inv": 1, "sign": 1, "eps": 1}
CONST_AT = dict(zip(CONST, np.cumsum([0] + list(CONST.values()))))
N_CONST = sum(CONST.values())

TWO_PI_A = 6.28125
TWO_PI_B = float(np.float32(np.round((2 * np.pi - TWO_PI_A) * 2**21) / 2**21))
TWO_PI_C = float(np.float32(2 * np.pi - TWO_PI_A - TWO_PI_B))
ROUND = 1.5 * 2.0**23
PI_BELOW = 3.1415925


class Plan:

    def __init__(self):
        self.place, self.start, self.end, self.units, self.norm = {}, {}, {}, 0, {}
        self.in_set, self.last, self.pending, self.sum_before = [0, 0], 1, {}, {}
        self.set_before = {}
        self.filled = {}
        self.weights = []
        self.group(("mem_keys", 0), FULL)
        self.sum_squares("mem")
        self.turn(("means", 0))
        self.group(("mem_values", 0), FULL)
        self.turn(("means", 1))
        for g in range(OUT_GROUPS):
            self.group(("pool", g), PAIR)
        self.group(("mem_values", 1), FULL)
        self.sum_squares("mixed0")
        self.group(("cross_q", 0), FULL)
        self.sum_squares("before_cross0")
        self.group(("mem_keys", 1), FULL)
        self.cross(0)
        self.ffn(0)
        for name in SPARSE:
            self.group(name, IDX_UNITS if name == "idx" else FULL)
            if name == ("iq", 0):
                self.sum_squares("before_mix1")
            for _, turn in BESIDE.get(name, ()):
                self.turn(turn, beside=True)
        for g in range(1, OUT_GROUPS):
            self.group(("att_out", g), FULL)
        self.sum_squares("mixed1")
        self.group(("cross_q", 1), FULL)
        self.sum_squares("before_cross1")
        self.cross(1)
        self.ffn(1)
        assert self.units == UNITS

    def _put(self, name, beside=False):
        which = 1 - self.last
        self.place[name] = which, self.in_set[which]
        self.in_set[which] += 1
        if beside:
            return
        self.last = which
        if self.last in self.pending:
            self.sum_before[name] = self.pending.pop(self.last)

    def group(self, name, units):
        self._put(name)
        self.start[name] = self.units
        self.units += units
        self.end[name] = self.units
        self.weights.append((name, units))

    def turn(self, name, beside=False):
        self._put(name, beside)
        self.filled[name] = len(self.filled) + 1

    def sum_squares(self, name):
        self.norm[name] = 1 - self.last, len(self.norm)
        self.set_before[name] = self.in_set[1 - self.last]
        self.pending[1 - self.last] = name

    def cross(self, l):
        self._put(("cross", l), beside=l == 0)
        for g in range(OUT_GROUPS):
            self.group(("cross_out", l, g), PAIR)
        self.sum_squares(f"crossed{l}")

    def ffn(self, l):
        self.group(("glu", l, 0), FULL)
        self.sum_squares(f"before_ffn{l}")
        for g in range(1, GLU_GROUPS):
            self.group(("glu", l, g), FULL)
        for g in range(OUT_GROUPS):
            self.group(("down", l, g), DOWN)
        self.sum_squares(f"ffn{l}")


SPARSE = (("iq", 0), "idx", ("iq", 1), ("iq", 2), ("iq", 3), "keys", "values", ("q", 0), ("q", 1), ("q", 2), ("q", 3),
          ("att_out", 0))
BESIDE = {
    ("iq", 1): ((3, ("weights", 0)), (5, ("logits", 0))), ("iq", 2): ((5, ("logits", 1)),), ("iq", 3): ((5, ("logits", 2)),),
    "keys": ((5, ("logits", 3)),), ("q", 1): ((5, ("scores", 0)),),
    ("q", 2): ((2, ("T", 0)), (3, ("o", 0)), (5, ("scores", 1))),
    ("q", 3): ((2, ("T", 1)), (3, ("o", 1)), (5, ("scores", 2))),
    ("att_out", 0): ((1, ("T", 2)), (2, ("o", 2)), (3, ("scores", 3)), (5, ("T", 3)), (6, ("o", 3))),
}
ROTATED = HEADS // BANKS + IDX_HEADS // BANKS + 1
SUMS = ("mem", "before_cross0", "before_ffn0", "before_mix1", "before_cross1", "before_ffn1")
ROW_SUMS = ("mem", "before_ffn0", "before_mix1", "before_ffn1", "mixed0", "crossed0", "ffn0", "mixed1", "crossed1", "ffn1")
TOKEN_SUMS = ("mem", "before_cross0", "before_mix1", "before_cross1")
Y_ADDED = OUT_GROUPS - 1
Y_SQUARED = OUT_GROUPS - 1 + BANKS
DVE_SCALES = BANKS
POOL_LEAD = 2
CROSS = (
    (("s", 0), ("s", 1), ("s", 2), ("s", 3), ("T", 0), ("T", 1), ("T", 2), ("T", 3), ("o", 0), ("o", 1), ("o", 2), ("o", 3)),
    (("s", 0), ("s", 1), ("s", 2), ("s", 3), ("T", 0), ("T", 1), ("T", 2), ("o", 0), ("T", 3), ("o", 1), ("o", 2), ("o", 3)),
)
MIXED = ("mixed0", "crossed0", "ffn0", "mixed1", "crossed1", "ffn1")


class Seen:

    def __init__(self, eng):
        self.eng, self.count = eng, {}

    def next(self, sem, k=1):
        self.count[sem.name] = self.count.get(sem.name, 0) + k
        self.eng.wait_ge(sem, self.count[sem.name])


def hybrid_trunk(nc, xT, x_tokens, memT, positions, averages, vectors, constants, weights, outT, kv_store):
    plan = Plan()
    place_of, start, end, norm = plan.place, plan.start, plan.end, plan.norm
    ctx = ExitStack()
    with ctx:
        at = [(nc.sbuf_base + 31) // 32 * 32]

        def place(name, shape, dt, offset=None):
            size = int(np.prod(shape[1:])) * 4
            if offset is None:
                offset = at[0]
                at[0] += (size + 31) // 32 * 32
            return nc.alloc_sbuf_tensor_at(name, shape, dt, offset=offset)

        def sem(name):
            return ctx.enter_context(nc.semaphore(name))

        K = 1024
        h = place("h", [P, C, T], F32)
        x_at = at[0]
        X = place("X", [P, C, 2 * T], F32R)
        raw = place("raw", [P, RING, UNIT], F32)
        w_hi = place("w_hi", [P, RING, UNIT], F32R)
        w_lo = place("w_lo", [P, RING, UNIT], F32R)
        low = place("low", [P, BANKS, T], F32)
        gu = place("gu", [P, BANKS, T], F32)
        sq = gu
        tail = at[0]
        squares = place("squares", [P, BANKS, T], F32)
        act_gate = place("act_gate", [P, 2, T], F32, tail)
        hid = place("hid", [P, 2, T], F32, tail + 2 * K)
        consts = place("consts", [P, N_CONST], F32)
        vec = place("vec", [P, N_GAINS, C], F32)
        x_square = place("x_square", [P, HALVES, D], F32, x_at)
        std = place("std", [P, T + HALVES], F32)
        rstd_post = place("rstd_post", [P, T], F32)
        rstd_pre = place("rstd_pre", [P, T + HALVES], F32)
        rstd_mem = place("rstd_mem", [P, T + HALVES], F32)
        hsum = place("hsum", [P, T], F32)
        cos = place("cos", [ROT, T], F32)
        sin = place("sin", [ROT, T], F32)
        iw = place("iw", [P, HALVES, IDX_HEADS], F32)
        x_rstd = place("x_rstd", [P, 3, HALVES], F32)
        query_scale = place("query_scale", [P, 2, HALVES], F32)
        warm = place("warm", [P, 32], F32)
        peak = place("peak", [P, 8], F32)
        npeak = place("npeak", [P, 8], F32)
        total = place("total", [P, 8], F32)
        rtotal = place("rtotal", [P, 8], F32)
        top8 = place("top8", [P, HALVES, 8], F32)

        base = at[0]
        at[0] += CF * 2 * K
        assert at[0] <= nc.sbuf_usable_end, (at[0], nc.sbuf_usable_end)
        hidden = place("hidden", [P, CF, 2 * T], F32R, base)
        y_mix = place("y_mix", [P, C, T], F32, base + 64 * K)
        y_ffn = place("y_ffn", [P, C, T], F32, x_at + 16 * K)
        kv = place("kv", [P, 2, BANKS, T], F32, base + 80 * K)
        XM = place("XM", [P, C, 2 * T], F32R, base)
        kv1 = place("kv1", [P, 2, BANKS, T], F32, base + 32 * K)
        average = place("average", [P, len(POOL_WINDOWS), REACH + P], F32, base + 40 * K)
        mem = place("mem", [P, C, T], F32, base + 48 * K)
        x_tok = place("x_tok", [P, HALVES, D], F32, base + 64 * K)
        ang = place("ang", [ROT, T], F32, base + 32 * K)
        turns_ = place("turns", [ROT, T], F32, base + 33 * K)
        red = place("red", [ROT, 2, T], F32, base + 34 * K)
        pos_i = place("pos_i", [ROT, T], I32, base + 36 * K)
        pos_f = place("pos_f", [ROT, T], F32, base + 37 * K)
        xq = place("xq", [P, X_HEADS, T], F32, base + 40 * K)
        xp = place("xp", [P, X_HEADS, HALVES, T], F32, base + 44 * K)
        xpT = place("xpT", [P, X_HEADS, HALVES, T], F32, base + 52 * K)
        quad = [place(f"quad{n}", [P, BANKS, T], F32, base + 4 * K * n) for n in range(2)]
        keys = place("keys", [P, KV_HEADS, T], F32, base + 8 * K)
        values = place("values", [P, HALVES, KV_HEADS * P], F32, base + 12 * K)
        ik = place("ik", [P, T], F32, base + 16 * K)
        iw_rows = place("iw_rows", [IDX_HEADS, T], F32, base + 26 * K)
        score = place("score", [P, KEYS], F32, base + 17 * K)
        work = place("work", [P, KEYS], F32, base + 18 * K + 512)
        mask = place("mask", [P, KEYS], F32, base + 20 * K)
        swap = place("swap", [ROT, BANKS, T], F32, base + 21 * K + 512)
        masked = place("masked", [P, BANKS, KEYS], F32, base + 26 * K)
        attended = place("attended", [P, HEADS, 2 * T], F32R, base + 32 * K)
        probs = place("probs", [P, BANKS, KEYS], F32, base + 64 * K)
        probsT = place("probsT", [P, BANKS, KEYS], F32, base + 70 * K)

        ps = ctx.enter_context(nc.psum_tensor("ps", [P, 2 * BANKS, 2 * T], F32))

        def const(name):
            return consts[:, CONST_AT[name]:CONST_AT[name] + CONST[name]]

        def bank_set(n):
            return ps[:, BANKS * n:BANKS * n + BANKS, :]

        def banks(name):
            return bank_set(place_of[name][0])

        def means_at(c):
            return banks(("means", c // 8))[:, c % 8 // 2, c % 2 * T:c % 2 * T + T]

        probs_before = 0, X_HEADS + 2 * (HEADS // BANKS)

        def over(row, n):
            return row.unsqueeze(1).to_broadcast([row.shape[0], n, T])

        ident, ones, causal = const("ident"), const("ones"), const("causal")

        landed = [sem(f"landed{n}") for n in range(RING)]
        hi_ready = sem("hi_ready")
        lo_ready = sem("lo_ready")
        units_used = sem("units_used")
        psum_filled = sem("psum_filled")
        set_read = [sem(f"set_read{n}") for n in range(2)]
        low_ready = sem("low_ready")
        bank_filled = sem("bank_filled")
        y_ready = sem("y_ready")
        y_squared = sem("y_squared")
        y_added = sem("y_added")
        ss_ready = sem("ss_ready")
        std_ready = sem("std_ready")
        x_squared = sem("x_squared")
        x_std_ready = sem("x_std_ready")
        x_normed = sem("x_normed")
        y_scaled = sem("y_scaled")
        h_ready = sem("h_ready")
        h_squared = sem("h_squared")
        h_added = sem("h_added")
        x_hi_ready = sem("x_hi_ready")
        x_ready = sem("x_ready")
        query_ready = sem("query_ready")
        swap_ready = sem("swap_ready")
        sin_done = sem("sin_done")
        q_ready = sem("q_ready")
        npeak_ready = sem("npeak_ready")
        scores_added = sem("scores_added")
        exp_ready = sem("exp_ready")
        probs_ready = sem("probs_ready")
        att_hi_ready = sem("att_hi_ready")
        last_heads = sem("last_heads")
        att_ready = sem("att_ready")
        mem_keys_out = sem("mem_keys_out")
        rstd_ready = sem("rstd_ready")
        gu_scaled = sem("gu_scaled")
        silu_ready = sem("silu_ready")
        hid_ready = sem("hid_ready")
        hid_hi_ready = sem("hid_hi_ready")
        hidden_ready = sem("hidden_ready")
        head_filled = sem("head_filled")
        head_T = sem("head_T")
        ang_ready = sem("ang_ready")
        rope_ready = sem("rope_ready")
        dve_step = sem("dve_step")
        consts_in = sem("consts_in")
        pos_in = sem("pos_in")
        mem_in = [sem(f"mem_in{n}") for n in range(MEM_PARTS)]
        x_in = sem("x_in")
        x_tok_in = [sem(f"x_tok_in{n}") for n in range(HALVES)]
        average_in = sem("average_in")
        kv_stored = sem("kv_stored")
        kv_loaded = sem("kv_loaded")
        out_done = sem("out_done")

        block = ctx.enter_context(nc.Block())

        def filled(eng, name):
            if name in end:
                eng.wait_ge(units_used, end[name])
            else:
                eng.wait_ge(psum_filled, plan.filled[name])

        def read_out(eng, name):
            which, n = place_of[name]
            eng.wait_ge(set_read[which], n + 1)

        def read_signal(name):
            return set_read[place_of[name][0]]

        @block.sync
        def _(sp):
            for n in range(MEM_PARTS):
                sp.dma_start(mem[:, 2 * n:2 * n + 2, :], memT[:, 2 * n:2 * n + 2, :]).then_inc(mem_in[n], 16)
                if n < RING:
                    sp.dma_start(raw[:, n, :], weights[n]).then_inc(landed[n], 16)
            for n in range(RING):
                sp.wait_ge(lo_ready, n + 1)
                sp.dma_start(raw[:, n, :], weights[RING + n]).then_inc(landed[n], 16)
                if n < HALVES:
                    sp.dma_start(x_tok[:, n, :], x_tokens[:, n, :]).then_inc(x_tok_in[n], 16)
                if n == HALVES:
                    sp.dma_start(average[:, :, :], averages).then_inc(average_in, 16)
            with sp.Fori(1, UNITS // RING - 1) as i:
                for n in range(RING):
                    sp.wait_ge(lo_ready, i * RING + (n + 1))
                    sp.dma_start(raw[:, n, :], weights[bass.ds(i * RING + (RING + n), 1)].squeeze(0)).then_inc(landed[n], 16)
            for lo, hi in OUT_PARTS:
                sp.wait_ge(h_ready, C * (len(MIXED) - 1) + hi)
                sp.dma_start(outT[:, lo:hi, :], h[:, lo:hi, :]).then_inc(out_done, 16)
            sp.wait_ge(out_done, 16 * len(OUT_PARTS))

        @block.gpsimd
        def _(pool):
            def add_square(n, c):
                pool.wait_ge(h_squared, C * n + c + 1)
                if c == 0:
                    nc.gpsimd.tensor_copy(hsum[:, :], sq[:, 0, :]).then_inc(h_added, 1)
                else:
                    pool.wait_ge(h_added, C * n + c)
                    nc.gpsimd.tensor_tensor(hsum[:, :], hsum[:, :], sq[:, c % BANKS, :], ALU.add).then_inc(h_added, 1)

            for c in range(C):
                add_square(0, c)
            for m, name in enumerate(MIXED):
                if name == "mixed1":
                    pool.wait_ge(rope_ready, 2)
                    for n in range(ROTATED):
                        pool.wait_ge(swap_ready, n + 1)
                        nc.gpsimd.tensor_tensor(swap[:, :, :], swap[:, :, :], over(sin[:, :], BANKS), ALU.mult).then_inc(sin_done, 1)
                pool.wait_ge(rstd_ready, norm[name][1] + 1)
                y = y_ffn if name.startswith("ffn") else y_mix
                for c in range(DVE_SCALES, C + DVE_SCALES + POOL_LEAD):
                    if c < C:
                        nc.gpsimd.tensor_tensor(y[:, c, :], y[:, c, :], rstd_post[:, :], ALU.mult).then_inc(y_scaled, 1)
                    done = c - DVE_SCALES - POOL_LEAD
                    if m + 1 < len(SUMS) and done >= 0:
                        if done == 0:
                            pool.wait_ge(ss_ready, norm[SUMS[m]][1] + 1)
                        add_square(m + 1, done)

        @block.scalar
        def _(act):
            seen = Seen(act)
            split = [0]
            last_low = [None]
            warmed = [0]

            def split_hi(u0, j):
                slot = j % RING
                act.wait_ge(landed[slot], u0 * 4 + 16 * (j // RING + 1))
                if not isinstance(u0, int) or u0 + j >= RING:
                    act.wait_ge(units_used, u0 + (j + 1 - RING))
                nc.scalar.activation(w_hi[:, slot, :], raw[:, slot, :], ACT.Copy).then_inc(hi_ready, 1)

            def split_until(n):
                while split[0] < min(n, UNITS):
                    split_hi(split[0] // RING * RING, split[0] % RING)
                    split[0] += 1

            def load_table(func):
                n = warmed[0]
                warmed[0] += 1
                nc.scalar.activation(warm[0:1, n:n + 1], ones[0:1, 0:1], func)

            def low_free():
                if last_low[0] is not None:
                    read_out(act, last_low[0])

            def low_out(name, n=BANKS):
                filled(act, name)
                low_free()
                last_low[0] = name
                nc.scalar.activation(low[:, 0:n, :], banks(name)[:, 0:n, T:2 * T], ACT.Copy).then_inc(low_ready, 1)

            def root(name):
                which, n = norm[name]
                act.wait_ge(ss_ready, n + 1)
                if n:
                    act.wait_ge(rstd_ready, n)
                cols = slice(0 if name in ROW_SUMS else T, T + HALVES if name in TOKEN_SUMS else T)
                nc.scalar.activation(std[:, cols], bank_set(which)[:, BANKS - 1, cols], ACT.Sqrt,
                                     scale=1.0 / D, bias=const("eps")).then_inc(std_ready, 1)

            def output_group(y, name, group, g, gain=None):
                short = end[group] - start[group] == PAIR and name != "mixed0"
                split_until(end[group] + (AHEAD if g < OUT_GROUPS - 1 - short else 0 if short and g == OUT_GROUPS - 1 else 2))
                scale = lambda b: 1.0 if gain is None else vec[:, gain, BANKS * g + b:BANKS * g + b + 1]
                m = MIXED.index(name)

                def square_group():
                    if g > 2:
                        act.wait_ge(y_added, m * Y_ADDED + g - 2)
                    nc.scalar.activation((sq if g > 1 else squares)[:, :, :], y[:, BANKS * (g - 1):BANKS * g, :],
                                         ACT.Square).then_inc(y_squared, 1)

                if g < OUT_GROUPS - 1:
                    if gain is None:
                        low_out(group)
                    else:
                        filled(act, group)
                        low_free()
                        last_low[0] = group
                        for b in range(BANKS):
                            ins = nc.scalar.activation(low[:, b, :], banks(group)[:, b, T:2 * T], ACT.Copy, scale=scale(b))
                        ins.then_inc(low_ready, 1)
                    if g:
                        square_group()
                    elif not name.startswith("crossed"):
                        load_table(ACT.Sqrt)
                    return
                low_free()
                last_low[0] = group
                for b in range(BANKS):
                    if b < BANKS - 1:
                        seen.next(bank_filled)
                    else:
                        filled(act, group)
                    nc.scalar.activation(low[:, b, :], banks(group)[:, b, T:2 * T], ACT.Copy, scale=scale(b)).then_inc(low_ready, 1)
                    if b == 0:
                        square_group()
                    if b == 1:
                        split_until(end[group] + 1)
                        act.wait_ge(y_added, m * Y_ADDED + OUT_GROUPS - 2)
                    for done in ([], [0], [1, 2], [3])[b]:
                        if done < BANKS - 1:
                            act.wait_ge(y_ready, m * (BANKS - 1) + done + 1)
                        else:
                            read_out(act, group)
                        nc.scalar.activation(sq[:, done, :], y[:, BANKS * g + done, :], ACT.Square).then_inc(y_squared, 1)

            def square_h(src, name, c):
                if c >= BANKS:
                    act.wait_ge(h_added, C * SUMS.index(name) + c - BANKS + 1)
                nc.scalar.activation(sq[:, c % BANKS, :], src, ACT.Square).then_inc(h_squared, 1)

            def residual(gain, name, split_after=range(LAG + 1, C // 2)):
                for c in range(C):
                    seen.next(h_ready)
                    nc.scalar.activation(X[:, c, 0:T], h[:, c, :], ACT.Copy,
                                         scale=vec[:, gain, c:c + 1]).then_inc(x_hi_ready, 1)
                    square_h(h[:, c, :], name, c)
                    if c % 2 and c // 2 in split_after:
                        split_until(split[0] + 1)

            act.dma_start(vec[:, :, :], vectors).then_inc(consts_in, 16)
            act.dma_start(consts[:, :], constants).then_inc(consts_in, 16)
            act.dma_start(pos_i[:, :], positions.to_broadcast([ROT, T])).then_inc(pos_in, 16)
            act.wait_ge(consts_in, 32)
            load_table(ACT.Sqrt)
            for c in range(C):
                if c % 2 == 0:
                    act.wait_ge(mem_in[c // 2], 16)
                nc.scalar.activation(XM[:, c, 0:T], mem[:, c, :], ACT.Copy,
                                     scale=vec[:, MEM_GAIN, c:c + 1]).then_inc(x_hi_ready, 1)
                if c == 0:
                    split_until(1)
                square_h(mem[:, c, :], "mem", c)
                if c % 2:
                    split_until(c // 2 + 1 if c // 2 < AHEAD else split[0] + 1)
            act.dma_start(h[:, :, :], xT).then_inc(x_in, 16)
            act.wait_ge(x_squared, HALVES)
            nc.scalar.activation(x_rstd[:, 1, :], x_rstd[:, 0, :], ACT.Sqrt, scale=1.0 / D, bias=const("eps")).then_inc(x_std_ready, 1)

            def means_out(n):
                filled(act, ("means", n))
                for c in range(8 * n, 8 * n + 8):
                    nc.scalar.activation(X[:, c, 0:T], means_at(c), ACT.Copy, scale=vec[:, 0, c:c + 1]).then_inc(x_hi_ready, 1)

            split_until(end["mem_keys", 0] + 2)
            low_out(("mem_keys", 0))
            root("mem")
            split_until(end["mem_keys", 0] + AHEAD)
            means_out(0)

            def memory_values(l):
                filled(act, ("mem_values", l))
                act.wait_ge(rstd_ready, 1)
                for th in range(HALVES):
                    ins = nc.scalar.activation((kv, kv1)[l][:, 1, 2 * th:2 * th + 2, :],
                                               banks(("mem_values", l))[:, th, :].rearrange("p (a t) -> p a t", a=2),
                                               ACT.Copy, scale=rstd_mem[:, T + th:T + th + 1])
                ins.then_inc(read_signal(("mem_values", l)), 1)

            split_until(end["mem_values", 0] + AHEAD)
            memory_values(0)
            means_out(1)
            act.wait_ge(ang_ready, 1)
            for n, table in enumerate((cos, sin)):
                nc.scalar.activation(table[:, :], red[:, n, :], ACT.Sin).then_inc(rope_ready, 1)
            for g in range(OUT_GROUPS):
                output_group(y_mix, "mixed0", ("pool", g), g, POOL_SCALE)
            split_until(start["mem_values", 1] + 6)
            root("mixed0")
            residual(2, "before_cross0", range(C // 2))
            memory_values(1)

            def cross_attention(l):
                split_until(end["cross_q", l] + 2)
                if l == 0:
                    root(f"before_cross{l}")
                filled(act, ("cross_q", l))
                low_free()
                last_low[0] = "cross_q", l
                for b in range(BANKS):
                    nc.scalar.activation(low[:, b, :], banks(("cross_q", l))[:, b, T:2 * T], ACT.Copy).then_inc(low_ready, 1)
                if l:
                    root(f"before_cross{l}")
                load_table(ACT.Exp)
                if l == 0:
                    split_until(end["cross_q", l] + AHEAD)
                name = ("cross", l)

                def head_T_out(hd):
                    act.wait_ge(head_filled, l * len(CROSS[0]) + CROSS[l].index(("T", hd)) + 1)
                    nc.scalar.activation(xpT[:, hd, :, :], banks(name)[:, hd, :].rearrange("p (m t) -> p m t", m=2),
                                         ACT.Copy).then_inc(head_T, 1)

                def head_out(hd):
                    act.wait_ge(head_filled, l * len(CROSS[0]) + CROSS[l].index(("o", hd)) + 1)
                    nc.scalar.activation(X[:, hd, 0:T], banks(name)[:, hd, 0:T], ACT.Copy).then_inc(att_hi_ready, 1)

                def head_exp(hd):
                    seen.next(npeak_ready)
                    for th in range(HALVES):
                        i = HALVES * hd + th
                        ins = nc.scalar.activation(xp[:, hd, th, :], banks(name)[:, hd, th * T:(th + 1) * T], ACT.Exp,
                                                   scale=query_scale[:, 0, th:th + 1], bias=npeak[:, i:i + 1],
                                                   accum_out=total[:, i:i + 1])
                    ins.then_inc(exp_ready, 1)

                if l == 0:
                    for hd in range(X_HEADS):
                        head_exp(hd)
                        split_until(split[0] + 1)
                    for hd in range(X_HEADS):
                        head_T_out(hd)
                    split_until(end["mem_keys", 1] + 2)
                else:
                    for hd in range(X_HEADS - 1):
                        head_exp(hd)
                    head_T_out(0)
                    head_exp(X_HEADS - 1)
                    for hd in range(1, X_HEADS):
                        head_T_out(hd)
                    split_until(end["cross_q", l] + AHEAD)
                for hd in range(X_HEADS):
                    head_out(hd)
                load_table(ACT.Sqrt)
                if l == 0:
                    split_until(end["mem_keys", 1] + AHEAD)
                    low_out(("mem_keys", 1))
                for g in range(OUT_GROUPS):
                    output_group(y_mix, f"crossed{l}", ("cross_out", l, g), g)
                root(f"crossed{l}")
                split_until(end["cross_out", l, OUT_GROUPS - 1] + AHEAD)
                residual(6 * l + 4, f"before_ffn{l}")

            def ffn(l):
                def glu(i, g, ahead=0):
                    which, n = place_of["glu", l, g]
                    before, m = place_of["glu", l, g - 1] if g else place_of["cross_out", l, OUT_GROUPS - 1]
                    act.wait_ge(units_used, i * (2 * FULL) + end["glu", l, g])
                    act.wait_ge(set_read[before], i + (m + 1))
                    nc.scalar.activation(low[:, :, :], bank_set(which)[:, :, T:2 * T], ACT.Copy).then_inc(low_ready, 1)
                    if ahead:
                        load_table(ACT.Silu)
                    split_until(split[0] + ahead)
                    act.wait_ge(gu_scaled, i * 2 + (l * GLU_GROUPS + g + 1))
                    nc.scalar.activation(act_gate[:, :, :], gu[:, 0:2, :], ACT.Silu).then_inc(silu_ready, 1)
                    split_until(split[0] + ahead)
                    act.wait_ge(hid_ready, i * 2 + (l * GLU_GROUPS + g + 1))
                    nc.scalar.activation(hidden[:, bass.ds(i * 4 + 2 * g, 2), 0:T], hid[:, :, :], ACT.Copy).then_inc(hid_hi_ready, 1)

                for g in range(2):
                    split_until(end["glu", l, g] + 2)
                    if g == 0:
                        root(f"before_ffn{l}")
                    split_until(end["glu", l, g] + AHEAD)
                    glu(0, g, 1 - g)
                with act.Fori(0, GLU_GROUPS // 2 - 1) as i:
                    for k in range(2):
                        for j in range(FULL):
                            split_hi(i * (2 * FULL) + split[0], FULL * k + j)
                        glu(i, 2 + k)
                split[0] += (GLU_GROUPS - 2) * FULL
                last_low[0] = "glu", l, GLU_GROUPS - 1
                for g in range(OUT_GROUPS):
                    if g == OUT_GROUPS - 1:
                        seen.count["bank_filled"] = seen.count.get("bank_filled", 0) + BANKS - 1
                    output_group(y_ffn, f"ffn{l}", ("down", l, g), g)
                root(f"ffn{l}")
                split_until(end["down", l, OUT_GROUPS - 1] + AHEAD)

            cross_attention(0)
            act.wait_ge(mem_keys_out, 2)
            read_out(act, ("mem_values", 1))
            act.dma_start(kv_store, kv1[:, :, :, :]).then_inc(kv_stored, 16)
            act.wait_ge(kv_stored, 16)
            ffn(0)
            residual(6, "before_mix1")

            act.dma_start(kv[:, :, :, :], kv_store).then_inc(kv_loaded, 16)
            def sparse_turn(name):
                what, g = name
                if what == "weights":
                    return
                if what == "logits":
                    filled(act, name)
                    if g:
                        act.wait_ge(scores_added, g)
                    nc.scalar.activation(masked[:, :, :], banks(name)[:, :, 0:KEYS], ACT.Relu, scale=SCALE).then_inc(read_signal(name), 1)
                elif what == "scores":
                    for i in range(HALVES * BANKS):
                        if i % BANKS == 0:
                            seen.next(npeak_ready)
                        b, th = divmod(i, HALVES)
                        cols = slice(0, P) if th == 0 else slice(P, KEYS)
                        ins = nc.scalar.activation(probs[:, b, cols], masked[:, b, cols], ACT.Exp,
                                                   scale=query_scale[:, 0, th:th + 1], bias=npeak[:, i:i + 1],
                                                   accum_out=total[:, i:i + 1])
                        if i % BANKS == BANKS - 1:
                            ins.then_inc(exp_ready, 1)
                            if g < 3:
                                split_until(split[0] + 1)
                elif what == "T":
                    filled(act, name)
                    nc.scalar.activation(probsT[:, :, :], banks(name)[:, :, 0:KEYS], ACT.Copy).then_inc(read_signal(name), 1)
                else:
                    filled(act, name)
                    for n, m in ((BANKS * g, BANKS),) if g < 3 else ((BANKS * g + b, 1) for b in range(BANKS)):
                        b = n % BANKS
                        nc.scalar.activation(attended[:, n:n + m, 0:T], banks(name)[:, b:b + m, 0:T], ACT.Copy).then_inc(att_hi_ready, 1)

            for name in SPARSE:
                for unit, turn in BESIDE.get(name, ()):
                    split_until(start[name] + unit + AHEAD)
                    sparse_turn(turn)
                if name == "values":
                    load_table(ACT.Exp)
                    split_until(end["values"] + AHEAD)
                    filled(act, "values")
                    act.wait_ge(rstd_ready, norm["before_mix1"][1] + 1)
                    for th in range(HALVES):
                        ins = nc.scalar.activation(values[:, th, :], banks("values")[:, th, :], ACT.Copy,
                                                   scale=rstd_pre[:, T + th:T + th + 1])
                    ins.then_inc(read_signal("values"), 1)
                elif name == "idx":
                    split_until(end[name] + 2)
                    filled(act, name)
                    low_free()
                    last_low[0] = name
                    nc.scalar.activation(low[:, 0, :], banks(name)[:, 0, T:2 * T], ACT.Copy)
                    nc.scalar.activation(low[0:IDX_HEADS, 1, :], banks(name)[0:IDX_HEADS, 1, T:2 * T], ACT.Copy).then_inc(low_ready, 1)
                elif name != ("att_out", 0):
                    split_until(end[name] + 2)
                    low_out(name)
                    if name == ("iq", 0):
                        root("before_mix1")
                    split_until(end[name] + AHEAD)
            for g in range(OUT_GROUPS):
                output_group(y_mix, "mixed1", ("att_out", g), g)
            root("mixed1")
            split_until(end["att_out", OUT_GROUPS - 1] + AHEAD)
            residual(6 + 2, "before_cross1")
            cross_attention(1)
            ffn(1)

        @block.vector
        def _(dve):
            seen = Seen(dve)
            split = [0]
            v = nc.vector

            def step(ins):
                ins.then_inc(dve_step, 1)
                seen.next(dve_step)

            def split_lo(u0, j):
                slot = j % RING
                dve.wait_ge(hi_ready, u0 + (j + 1))
                v.tensor_tensor(w_lo[:, slot, :], raw[:, slot, :], w_hi[:, slot, :].bitcast(F32), ALU.subtract).then_inc(lo_ready, 1)

            def split_until(n):
                while split[0] < min(n, UNITS):
                    split_lo(split[0] // RING * RING, split[0] % RING)
                    split[0] += 1

            def add_low(out, name, n=BANKS):
                seen.next(low_ready)
                v.tensor_tensor(out, banks(name)[:, 0:n, 0:T], low[:, 0:n, :], ALU.add).then_inc(read_signal(name), 1)
                read_out(dve, name)

            def one_over_root(name, out):
                n = norm[name][1]
                cols = slice(0 if name in ROW_SUMS else T, T + HALVES if name in TOKEN_SUMS else T)
                dve.wait_ge(std_ready, n + 1)
                v.reciprocal(out[:, cols], std[:, cols]).then_inc(rstd_ready, 1)
                dve.wait_ge(rstd_ready, n + 1)

            def x_low(src, gain, c, out, wait=1, signal=x_ready):
                if wait:
                    seen.next(x_hi_ready, wait)
                v.scalar_tensor_tensor(out[:, c, T:2 * T], src, vec[:, gain, c:c + 1],
                                       out[:, c, 0:T].bitcast(F32), ALU.mult, ALU.subtract).then_inc(signal, 1)

            def output_group(y, name, group, g, gain=None):
                short = end[group] - start[group] == PAIR and name != "mixed0"
                split_until(end[group] + (AHEAD if g < OUT_GROUPS - 1 - short else 0 if short and g == OUT_GROUPS - 1 else 2))
                per_bank = g == OUT_GROUPS - 1
                out = banks(group)

                def add_bank(b):
                    c = BANKS * g + b
                    if gain is None:
                        return v.tensor_tensor(y[:, c, :], out[:, b, 0:T], low[:, b, :], ALU.add)
                    return v.scalar_tensor_tensor(y[:, c, :], out[:, b, 0:T], vec[:, gain, c:c + 1], low[:, b, :], ALU.mult, ALU.add)

                def add_squares():
                    seen.next(y_squared)
                    if g > 1:
                        v.tensor_tensor(squares[:, :, :], squares[:, :, :], sq[:, :, :], ALU.add).then_inc(y_added, 1)
                        seen.next(y_added)

                if not per_bank:
                    if gain is None:
                        add_low(y[:, BANKS * g:BANKS * g + BANKS, :], group)
                    else:
                        seen.next(low_ready)
                        for b in range(BANKS):
                            ins = add_bank(b)
                        ins.then_inc(read_signal(group), 1)
                        read_out(dve, group)
                    if g:
                        add_squares()
                    return
                for b in range(BANKS):
                    seen.next(low_ready)
                    add_bank(b).then_inc(y_ready if b < BANKS - 1 else read_signal(group), 1)
                    if b == 0:
                        add_squares()
                    if b == BANKS - 2:
                        step(v.tensor_tensor(squares[:, 0:2, :], squares[:, 0:2, :], squares[:, 2:4, :], ALU.add))
                        v.tensor_tensor(squares[:, 0, :], squares[:, 0, :], squares[:, 1, :], ALU.add).then_inc(y_added, 1)
                        seen.next(y_added)
                seen.next(y_ready, BANKS - 1)
                read_out(dve, group)
                seen.next(y_squared, BANKS)

            def residual(y, name, gain, next_gain=None, split_after=range(LAG, C // 2)):
                one_over_root(name, rstd_post)
                done = MIXED.index(name) * C
                for c in range(C):
                    if c < DVE_SCALES:
                        step(v.tensor_tensor(y[:, c, :], y[:, c, :], rstd_post[:, :], ALU.mult))
                    else:
                        seen.next(y_scaled)
                    v.scalar_tensor_tensor(h[:, c, :], y[:, c, :], vec[:, gain, c:c + 1], h[:, c, :],
                                           ALU.mult, ALU.add).then_inc(h_ready, 1)
                    if next_gain is None:
                        continue
                    if c:
                        dve.wait_ge(h_ready, done + c)
                        x_low(h[:, c - 1, :], next_gain, c - 1, X)
                    if c == C - 1:
                        dve.wait_ge(h_ready, done + C)
                        x_low(h[:, c, :], next_gain, c, X)
                    if c % 2 and c // 2 in split_after:
                        split_until(split[0] + 1)

            swapped_rows = [(r + ROT // 2) % ROT for r in range(ROT)]

            def rotate(q, n):
                src, dst = q[0:ROT], swap[:, 0:n, :]
                if n == 1:
                    step(v.stream_shuffle(dst, src, swapped_rows))
                    step(v.tensor_tensor(dst, dst, over(sin[:, :], n), ALU.mult))
                    step(v.tensor_tensor(src, src, over(cos[:, :], n), ALU.mult))
                else:
                    v.stream_shuffle(dst, src, swapped_rows).then_inc(swap_ready, 1)
                    seen.next(swap_ready)
                    step(v.tensor_tensor(src, src, over(cos[:, :], n), ALU.mult))
                    split_until(split[0] + 1)
                    seen.next(sin_done)
                v.tensor_tensor(src, src, dst, ALU.add).then_inc(q_ready, 1)
                seen.next(q_ready)

            dve.wait_ge(consts_in, 32)
            for c in range(C):
                if c % 2 == 0:
                    dve.wait_ge(mem_in[c // 2], 16)
                x_low(mem[:, c, :], MEM_GAIN, c, XM)
                if c == 0:
                    split_until(1)
                if c % 2:
                    split_until(c // 2 + 1 if c // 2 < AHEAD else split[0] + 1)
                if c in (C - 7, C - 3):
                    th = c // (C - 3)
                    dve.wait_ge(x_tok_in[th], 16)
                    v.tensor_tensor_reduce(x_square[:, th, :], x_tok[:, th, :], x_tok[:, th, :], 1.0, 0.0,
                                           ALU.mult, ALU.add, x_rstd[:, 0, th:th + 1]).then_inc(x_squared, 1)
            dve.wait_ge(x_std_ready, 1)
            step(v.reciprocal(x_rstd[:, 2, :], x_rstd[:, 1, :]))
            for th in range(HALVES):
                v.tensor_scalar(x_tok[:, th, :], x_tok[:, th, :], x_rstd[:, 2, th:th + 1], None, ALU.mult).then_inc(x_normed, 1)
            def rotary_angles():
                dve.wait_ge(pos_in, 16)
                step(v.tensor_copy(pos_f[:, :], pos_i[:, :]))
                step(v.tensor_scalar(ang[:, :], pos_f[:, :], const("inv")[0:ROT, :], None, ALU.mult))
                for n, quarter in enumerate((0.25, 0.0)):
                    r = red[:, n, :]
                    step(v.tensor_scalar(turns_[:, :], ang[:, :], float(1 / (2 * np.pi)), quarter, ALU.mult, ALU.add))
                    step(v.tensor_scalar(turns_[:, :], turns_[:, :], ROUND, None, ALU.add))
                    step(v.tensor_scalar(turns_[:, :], turns_[:, :], -ROUND, None, ALU.add))
                    step(v.scalar_tensor_tensor(r, turns_[:, :], -TWO_PI_A, ang[:, :], ALU.mult, ALU.add))
                    step(v.scalar_tensor_tensor(r, turns_[:, :], -TWO_PI_B, r, ALU.mult, ALU.add))
                    step(v.scalar_tensor_tensor(r, turns_[:, :], -TWO_PI_C, r, ALU.mult, ALU.add))
                    if quarter:
                        step(v.tensor_scalar(r, r, float(np.pi / 2), PI_BELOW, ALU.add, ALU.min))
                    else:
                        step(v.tensor_scalar(r, r, PI_BELOW, None, ALU.min))
                    step(v.tensor_scalar(r, r, -PI_BELOW, None, ALU.max))
                v.tensor_scalar(red[:, 1, :], red[:, 1, :], const("sign")[0:ROT, :], None, ALU.mult).then_inc(ang_ready, 1)

            def memory_keys(l):
                keys_out = (kv, kv1)[l][:, 0, :, :]
                add_low(keys_out, ("mem_keys", l))
                if l == 0:
                    one_over_root("mem", rstd_mem)
                v.tensor_tensor(keys_out, keys_out, over(rstd_mem[:, 0:T], BANKS), ALU.mult).then_inc(mem_keys_out, 1)

            def means_out(n):
                for c in range(8 * n, 8 * n + 8):
                    x_low(means_at(c), 0, c, X, 2 - c % 2 * 2, read_signal(("means", n)) if c % 8 == 7 else x_ready)

            split_until(end["mem_keys", 0] + 2)
            memory_keys(0)
            split_until(end["mem_keys", 0] + AHEAD)
            means_out(0)
            split_until(start["mem_values", 0] + 7)
            rotary_angles()
            split_until(end["mem_values", 0] + AHEAD)
            means_out(1)
            dve.wait_ge(x_in, 16)
            for g in range(OUT_GROUPS):
                output_group(y_mix, "mixed0", ("pool", g), g, POOL_SCALE)
            split_until(start["mem_values", 1] + 6)
            residual(y_mix, "mixed0", 1, 2, range(1, C // 2))

            def query_scales():
                step(v.tensor_scalar(query_scale[:, 0, :], rstd_pre[:, T:T + HALVES], SCALE, None, ALU.mult))
                step(v.tensor_scalar(query_scale[:, 1, :], rstd_pre[:, T:T + HALVES], -SCALE, None, ALU.mult))

            def normalise(p, i, n, signal):
                step(v.reciprocal(rtotal[:, i:i + n], total[:, i:i + n]))
                for i in range(i, i + n):
                    ins = v.tensor_scalar(p(i), p(i), rtotal[:, i:i + 1], None, ALU.mult)
                ins.then_inc(signal, 1)
                seen.next(signal)

            def cross_attention(l):
                split_until(end["cross_q", l] + 2)
                name = "cross_q", l
                for hd in range(X_HEADS):
                    seen.next(low_ready)
                    v.tensor_tensor(xq[:, hd, :], banks(name)[:, hd, 0:T], low[:, hd, :],
                                    ALU.add).then_inc(query_ready if hd < X_HEADS - 1 else read_signal(name), 1)
                one_over_root(f"before_cross{l}", rstd_pre)
                query_scales()
                if l == 0:
                    split_until(end["cross_q", l] + AHEAD)
                name = "cross", l

                def order(what, hd):
                    return l * len(CROSS[0]) + CROSS[l].index((what, hd)) + 1

                def head_peak(hd):
                    i = HALVES * hd
                    dve.wait_ge(head_filled, order("s", hd))
                    step(v.reduce_max(peak[:, i:i + HALVES], banks(name)[:, hd, :].rearrange("p (t m) -> p t m", t=HALVES), AX_X))
                    v.tensor_tensor(npeak[:, i:i + HALVES], peak[:, i:i + HALVES], query_scale[:, 1, :], ALU.mult).then_inc(npeak_ready, 1)

                def head_probs(hd):
                    seen.next(exp_ready)
                    normalise(lambda i: xp[:, i // HALVES, i % HALVES, :], HALVES * hd, HALVES, probs_ready)

                for hd in range(X_HEADS):
                    head_peak(hd)
                    if hd:
                        head_probs(hd - 1)
                        if l == 0:
                            split_until(split[0] + 1)
                head_probs(X_HEADS - 1)
                if l == 0:
                    split_until(end["mem_keys", 1] + 2)
                for hd in range(X_HEADS):
                    seen.next(att_hi_ready)
                    v.tensor_tensor(X[:, hd, T:2 * T], banks(name)[:, hd, 0:T], X[:, hd, 0:T].bitcast(F32),
                                    ALU.subtract).then_inc(att_ready if hd < X_HEADS - 1 else read_signal(name), 1)
                if l == 0:
                    split_until(end["mem_keys", 1] + AHEAD)
                    memory_keys(1)
                else:
                    split_until(end["cross_q", l] + AHEAD)
                for g in range(OUT_GROUPS):
                    output_group(y_mix, f"crossed{l}", ("cross_out", l, g), g)
                split_until(end["cross_out", l, OUT_GROUPS - 1] + 1)
                residual(y_mix, f"crossed{l}", 6 * l + 3, 6 * l + 4, range(C // 2))

            def ffn(l):
                low_before = seen.count["low_ready"]

                def glu(i, g, ahead=0):
                    which, n = place_of["glu", l, g]
                    out = bank_set(which)
                    dve.wait_ge(low_ready, i * 2 + (low_before + g + 1))
                    if l or g:
                        dve.wait_ge(hidden_ready, i * 2 + (l * GLU_GROUPS + g))
                    v.tensor_tensor(gu[:, :, :], out[:, :, 0:T], low[:, :, :], ALU.add).then_inc(set_read[which], 1)
                    dve.wait_ge(set_read[which], i + (n + 1))
                    split_until(split[0] + ahead)
                    v.tensor_tensor(gu[:, :, :], gu[:, :, :], over(rstd_pre[:, 0:T], BANKS), ALU.mult).then_inc(gu_scaled, 1)
                    split_until(split[0] + ahead)
                    dve.wait_ge(gu_scaled, i * 2 + (l * GLU_GROUPS + g + 1))
                    dve.wait_ge(silu_ready, i * 2 + (l * GLU_GROUPS + g + 1))
                    v.tensor_tensor(hid[:, :, :], act_gate[:, :, :], gu[:, 2:4, :], ALU.mult).then_inc(hid_ready, 1)
                    dve.wait_ge(hid_ready, i * 2 + (l * GLU_GROUPS + g + 1))
                    dve.wait_ge(hid_hi_ready, i * 2 + (l * GLU_GROUPS + g + 1))
                    v.tensor_tensor(hidden[:, bass.ds(i * 4 + 2 * g, 2), T:2 * T], hid[:, :, :],
                                    hidden[:, bass.ds(i * 4 + 2 * g, 2), 0:T].bitcast(F32), ALU.subtract).then_inc(hidden_ready, 1)

                for g in range(2):
                    split_until(end["glu", l, g] + 2)
                    if g == 0:
                        one_over_root(f"before_ffn{l}", rstd_pre)
                    split_until(end["glu", l, g] + AHEAD)
                    glu(0, g, 1 - g)
                with dve.Fori(0, GLU_GROUPS // 2 - 1) as i:
                    for k in range(2):
                        for j in range(FULL):
                            split_lo(i * (2 * FULL) + split[0], FULL * k + j)
                        glu(i, 2 + k)
                split[0] += (GLU_GROUPS - 2) * FULL
                seen.count["low_ready"] += GLU_GROUPS
                dve.wait_ge(hidden_ready, (l + 1) * GLU_GROUPS)
                for g in range(OUT_GROUPS):
                    output_group(y_ffn, f"ffn{l}", ("down", l, g), g)

            cross_attention(0)
            ffn(0)
            residual(y_ffn, "ffn0", 5, 6)

            dve.wait_ge(rope_ready, 2)

            def index_keys():
                split_until(end["idx"] + 1)
                seen.next(low_ready)
                step(v.tensor_tensor(ik[:, :], banks("idx")[:, 0, 0:T], low[:, 0, :], ALU.add))
                v.tensor_tensor(iw_rows[:, :], banks("idx")[0:IDX_HEADS, 1, 0:T], low[0:IDX_HEADS, 1, :],
                                ALU.add).then_inc(read_signal("idx"), 1)
                read_out(dve, "idx")
                split_until(end["idx"] + AHEAD)
                step(v.tensor_tensor(ik[:, :], ik[:, :], rstd_pre[:, 0:T], ALU.mult))
                rotate(ik[:, :].unsqueeze(1), 1)

            def heads_out(q, name):
                split_until(end[name] + 2)
                add_low(q[:, :, :], name)
                if name == ("iq", 0):
                    one_over_root("before_mix1", rstd_pre)
                split_until(end[name] + AHEAD)
                if name == "keys":
                    step(v.tensor_tensor(q[:, :, :], q[:, :, :], over(rstd_pre[:, 0:T], BANKS), ALU.mult))
                    split_until(split[0] + 1)
                rotate(q, BANKS)

            def take_8():
                for th, cols in enumerate((slice(0, P), slice(P, KEYS))):
                    step(v.max(top8[:, th, :], work[:, cols]))
                    step(v.match_replace(work[:, cols], top8[:, th, :], work[:, cols], TAKEN))

            def sparse_turn(name):
                what, g = name
                if what == "weights":
                    filled(dve, name)
                    for th in range(HALVES):
                        ins = v.tensor_scalar(iw[:, th, :], banks(name)[:, th, 0:IDX_HEADS], rstd_pre[:, T + th:T + th + 1], IW_SCALE,
                                              ALU.mult, ALU.mult)
                    ins.then_inc(read_signal(name), 1)
                    read_out(dve, name)
                    for th in range(HALVES):
                        step(v.tensor_scalar(iw[:, th, :], iw[:, th, :], rstd_pre[:, T + th:T + th + 1], None, ALU.mult))
                    query_scales()
                elif what == "logits":
                    read_out(dve, name)
                    for b in range(BANKS):
                        for th, cols in enumerate((slice(0, P), slice(P, KEYS))):
                            hd = BANKS * g + b
                            ins = v.scalar_tensor_tensor(score[:, cols], masked[:, b, cols], iw[:, th, hd:hd + 1], score[:, cols],
                                                         ALU.mult, ALU.add)
                            if th == 1 and b == BANKS - 1:
                                ins.then_inc(scores_added, 1)
                                seen.next(scores_added)
                            else:
                                step(ins)
                elif what == "scores":
                    filled(dve, name)
                    for i in range(HALVES * BANKS):
                        b, th = divmod(i, HALVES)
                        cols = slice(0, P) if th == 0 else slice(P, KEYS)
                        ins = v.tensor_tensor_reduce(masked[:, b, cols], banks(name)[:, b, cols], mask[:, cols], 1.0, TAKEN,
                                                     ALU.add, ALU.max, peak[:, i:i + 1])
                        if i % BANKS == BANKS - 1:
                            if b == BANKS - 1:
                                ins.then_inc(read_signal(name), 1)
                                read_out(dve, name)
                            else:
                                step(ins)
                            rows = slice(i - BANKS + 1, i + 1)
                            v.tensor_tensor(npeak[:, rows].rearrange("p (b t) -> p b t", t=HALVES),
                                            peak[:, rows].rearrange("p (b t) -> p b t", t=HALVES),
                                            query_scale[:, 1, :].unsqueeze(1).to_broadcast([P, BANKS // HALVES, HALVES]),
                                            ALU.mult).then_inc(npeak_ready, 1)
                    for half in range(2):
                        seen.next(exp_ready)
                        normalise(lambda i: probs[:, i // HALVES, slice(0, P) if i % HALVES == 0 else slice(P, KEYS)],
                                  half * BANKS, BANKS, probs_ready)
                        if g < 3:
                            split_until(split[0] + 1)
                elif what == "o":
                    for n, m in ((BANKS * g, BANKS),) if g < 3 else ((BANKS * g + b, 1) for b in range(BANKS)):
                        seen.next(att_hi_ready)
                        out, b = attended[:, n:n + m], n % BANKS
                        v.tensor_tensor(out[:, :, T:2 * T], banks(name)[:, b:b + m, 0:T], out[:, :, 0:T].bitcast(F32),
                                        ALU.subtract).then_inc(read_signal(name) if b + m == BANKS else last_heads, 1)

            step(v.memset(score[:, :], 0.0))
            for name in SPARSE:
                for unit, turn in BESIDE.get(name, ()):
                    split_until(start[name] + unit + AHEAD)
                    sparse_turn(turn)
                if name == "values":
                    step(v.tensor_tensor(work[:, :], score[:, :], causal, ALU.add))
                    for _ in range(TOPK // 8):
                        split_until(split[0] + 1)
                        take_8()
                    step(v.tensor_scalar(mask[:, :], work[:, :], TAKEN_BELOW, NEG, ALU.is_gt, ALU.mult))
                    step(v.tensor_tensor(mask[:, :], mask[:, :], causal, ALU.add))
                elif name == "idx":
                    index_keys()
                elif name == "keys":
                    heads_out(keys, name)
                elif name[0] in ("iq", "q"):
                    heads_out(quad[name[1] % 2], name)
            for g in range(OUT_GROUPS):
                output_group(y_mix, "mixed1", ("att_out", g), g)
            residual(y_mix, "mixed1", 6 + 1, 6 + 2)
            cross_attention(1)
            ffn(1)
            residual(y_ffn, "ffn1", 6 + 5)

        @block.tensor
        def _(pe):
            seen = Seen(pe)
            mm = nc.tensor.matmul

            def set_free(name, i=0):
                which, n = place_of[name]
                if n:
                    pe.wait_ge(set_read[which], i + n)

            def sum_squares(name):
                which, n = norm[name]
                out = bank_set(which)[:, BANKS - 1, :]
                if plan.set_before[name]:
                    pe.wait_ge(set_read[which], plan.set_before[name])
                if name in MIXED:
                    m = MIXED.index(name)
                    for b in range(BANKS):
                        if b == BANKS - 1:
                            pe.wait_ge(y_added, (m + 1) * Y_ADDED)
                            mm(out[:, 0:T], ones, squares[:, 0, :], start=False, stop=False)
                        pe.wait_ge(y_squared, m * Y_SQUARED + OUT_GROUPS + b)
                        ins = mm(out[:, 0:T], ones, sq[:, b, :], start=b == 0, stop=b == BANKS - 1)
                else:
                    pe.wait_ge(h_added, (SUMS.index(name) + 1) * C)
                    if name in ROW_SUMS:
                        ins = mm(out[:, 0:T], ones, hsum[:, :], start=True, stop=True)
                if name in TOKEN_SUMS:
                    for th in range(HALVES):
                        ins = mm(out[:, T + th:T + th + 1], hsum[:, th * P:th * P + P], ones[:, 0:1], start=True, stop=True)
                ins.then_inc(ss_ready, 1)

            def group(name, units, x, x_wait=None, i=0, unit_step=0, between={}, bank_by_bank=False):
                set_free(name, i)
                out, u0 = banks(name), start[name]

                def product(j, kk, b):
                    k, slot = 2 * j + kk, (u0 + j) % RING
                    if k == 0 and b == BANKS - 1 and name in plan.sum_before:
                        pe.wait_ge(std_ready, norm[plan.sum_before[name]][1] + 1)
                    w = slice(kk * BANKS * P + b * P, kk * BANKS * P + b * P + P)
                    mm(out[:, b, :], w_hi[:, slot, w], x(k), start=k == 0, stop=False)
                    return mm(out[:, b, T:2 * T], w_lo[:, slot, w], x(k)[:, 0:T], start=False, stop=k == 2 * units - 1)

                def arrived(j):
                    pe.wait_ge(lo_ready, (i * unit_step if unit_step else 0) + (u0 + j + 1))

                for j in range(units - 2 if bank_by_bank else units):
                    if j in between:
                        between[j]()
                    arrived(j)
                    for kk in range(2):
                        if x_wait:
                            x_wait(2 * j + kk)
                        for b in range(BANKS):
                            ins = product(j, kk, b)
                    ins.then_inc(units_used, 1)
                if bank_by_bank:
                    for b in range(BANKS):
                        for j in range(units - 2, units):
                            if b == 0:
                                arrived(j)
                            for kk in range(2):
                                if b == 0 and x_wait:
                                    x_wait(2 * j + kk)
                                ins = product(j, kk, b)
                        if b < BANKS - 1:
                            ins.then_inc(bank_filled, 1)
                    ins.then_inc(units_used, 2)

            def named(name, x, x_wait=None, **more):
                group(name, end[name] - start[name], x, x_wait, **more)

            def tokens_product(out, x, w_h, w_l, first, last):
                for th in range(HALVES):
                    o = out(th)
                    hi = x[:, th * P:th * P + P]
                    mm(o, hi, w_h, start=first, stop=False)
                    mm(o, hi, w_l, start=False, stop=False)
                    ins = mm(o, x[:, T + th * P:T + th * P + P], w_h, start=False, stop=last)
                return ins

            def token_group(name, x, between={}):
                set_free(name)
                for j in range(FULL):
                    if j in between:
                        between[j]()
                    u = start[name] + j
                    pe.wait_ge(lo_ready, u + 1)
                    for kk in range(2):
                        k = 2 * j + kk
                        w = slice(kk * BANKS * P, (kk + 1) * BANKS * P)
                        ins = tokens_product(lambda th: banks(name)[:, th, :], x(k), w_hi[:, u % RING, w], w_lo[:, u % RING, w],
                                             k == 0, k == C - 1)
                    ins.then_inc(units_used, 1)

            def in_X(k):
                return X[:, k, :]

            def in_XM(k):
                return XM[:, k, :]

            def in_attended(k):
                return attended[:, k, :]

            def next_x(k):
                seen.next(x_ready)

            def means(n):
                name = "means", n
                set_free(name)
                if n == 0:
                    pe.wait_ge(average_in, 16)
                    pe.wait_ge(x_normed, HALVES)
                for c in range(8 * n, 8 * n + 8):
                    if c == 8 * n + 6 and name in plan.sum_before:
                        pe.wait_ge(std_ready, norm[plan.sum_before[name]][1] + 1)
                    a, out = average[:, c // BANKS, :], means_at(c)
                    mm(out[:, 0:REACH], x_tok[:, 0, c * P:c * P + P], a[:, 0:REACH], start=True, stop=False, skip_group_check=True)
                    mm(out[:, P:REACH], x_tok[:, 1, c * P:c * P + P], a[:, REACH:REACH + REACH - P], start=False, stop=False,
                       skip_group_check=True)
                    ins = mm(out[:, REACH:T], x_tok[:, 1, c * P:c * P + P], a[:, 2 * REACH - P:REACH + P], start=False, stop=True,
                             skip_group_check=True)
                ins.then_inc(psum_filled, 1)

            pe.wait_ge(consts_in, 32)
            named(("mem_keys", 0), in_XM, next_x)
            sum_squares("mem")
            means(0)
            token_group(("mem_values", 0), in_XM)
            means(1)
            def mean_there(c):
                if c % 8 == 7:
                    read_out(pe, ("means", c // 8))
                else:
                    seen.next(x_ready)

            for g in range(OUT_GROUPS):
                named(("pool", g), lambda k: X[:, BANKS * g + k, :], lambda k: mean_there(BANKS * g + k),
                      bank_by_bank=g == OUT_GROUPS - 1)
            token_group(("mem_values", 1), in_XM, {2: lambda: sum_squares("mixed0")})

            def cross_attention(l):
                name = "cross", l
                out = banks(name)

                def scores():
                    set_free(name)
                    if l:
                        pe.wait_ge(kv_loaded, 16)
                    else:
                        pe.wait_ge(mem_keys_out, 1)
                    for hd in range(X_HEADS):
                        if hd < X_HEADS - 1:
                            pe.wait_ge(query_ready, l * (X_HEADS - 1) + hd + 1)
                        else:
                            read_out(pe, ("cross_q", l))
                        if hd == BANKS - 1 and name in plan.sum_before:
                            pe.wait_ge(std_ready, norm[plan.sum_before[name]][1] + 1)
                        for th in range(HALVES):
                            ins = mm(out[:, hd, th * T:th * T + T], xq[:, hd, th * P:th * P + P], kv[:, 0, hd, :], start=True, stop=True)
                        ins.then_inc(head_filled, 1)

                def transposed(hd):
                    pe.wait_ge(probs_ready, probs_before[l] + hd + 1)
                    for m in range(2):
                        for th in range(HALVES):
                            ins = nc.tensor.transpose(out[:, hd, m * T + th * P:m * T + th * P + P],
                                                      xp[:, hd, th, m * P:m * P + P], ident)
                    ins.then_inc(head_filled, 1)

                def output(hd):
                    pe.wait_ge(head_T, l * X_HEADS + hd + 1)
                    for m in range(2):
                        ins = mm(out[:, hd, 0:T], kv[:, 1, 2 * m + hd // 2, hd % 2 * P:hd % 2 * P + P], xpT[:, hd, m, :],
                                 start=m == 0, stop=m == 1)
                    ins.then_inc(head_filled, 1)

                named(("cross_q", l), in_X, next_x)
                sum_squares(f"before_cross{l}")
                if l == 0:
                    named(("mem_keys", 1), in_XM, between={
                        2: scores, 6: lambda: [transposed(hd) for hd in range(X_HEADS)],
                        7: lambda: [output(hd) for hd in range(X_HEADS)]})
                else:
                    scores()
                    for what, hd in CROSS[l][X_HEADS:]:
                        (transposed if what == "T" else output)(hd)

                def attention_there(k):
                    if k < X_HEADS - 1:
                        pe.wait_ge(att_ready, l * (X_HEADS - 1) + k + 1)
                    else:
                        read_out(pe, name)

                for g in range(OUT_GROUPS):
                    named(("cross_out", l, g), in_X, attention_there if g == 0 else None, bank_by_bank=g == OUT_GROUPS - 1)
                sum_squares(f"crossed{l}")

            def ffn(l):
                named(("glu", l, 0), in_X, next_x)
                sum_squares(f"before_ffn{l}")
                named(("glu", l, 1), in_X)
                with pe.Fori(0, GLU_GROUPS // 2 - 1) as i:
                    for k in range(2):
                        group(("glu", l, 2 + k), FULL, in_X, i=i, unit_step=2 * FULL)

                def hidden_there(k):
                    if k % 2 == 0:
                        pe.wait_ge(hidden_ready, l * GLU_GROUPS + k // 2 + 1)

                with pe.Fori(0, OUT_GROUPS // 2) as i:
                    for k in range(2):
                        group(("down", l, k), DOWN, lambda c: hidden[:, c, :], hidden_there if k == 0 else None,
                              i=i, unit_step=2 * DOWN, bank_by_bank=k == 1)
                sum_squares(f"ffn{l}")

            cross_attention(0)
            ffn(0)

            def index_group():
                set_free("idx")
                out = banks("idx")
                for j in range(IDX_UNITS):
                    u = start["idx"] + j
                    pe.wait_ge(lo_ready, u + 1)
                    for kk in range(4):
                        k = 4 * j + kk
                        w = slice(kk * 2 * P, kk * 2 * P + P)
                        mm(out[:, 0, :], w_hi[:, u % RING, w], X[:, k, :], start=k == 0, stop=False)
                        mm(out[:, 0, T:2 * T], w_lo[:, u % RING, w], X[:, k, 0:T], start=False, stop=k == C - 1)
                        w = slice(kk * 2 * P + P, kk * 2 * P + P + IDX_HEADS)
                        mm(out[0:IDX_HEADS, 1, :], w_hi[:, u % RING, w], X[:, k, :], start=k == 0, stop=False)
                        ins = mm(out[0:IDX_HEADS, 1, T:2 * T], w_lo[:, u % RING, w], X[:, k, 0:T], start=False, stop=k == C - 1)
                    ins.then_inc(units_used, 1)

            def query_key(name, q, k):
                set_free(name)
                seen.next(q_ready, 2 if name[1] == 0 else 1)
                for b in range(BANKS):
                    mm(banks(name)[:, b, 0:P], q[:, b, 0:P], k[:, 0:P], start=True, stop=True)
                    ins = mm(banks(name)[:, b, P:KEYS], q[:, b, P:T], k, start=True, stop=True)
                ins.then_inc(psum_filled, 1)

            def sparse_turn(name):
                what, g = name
                if what == "weights":
                    set_free(name)
                    for th in range(HALVES):
                        ins = nc.tensor.transpose(banks(name)[:, th, 0:IDX_HEADS], iw_rows[:, th * P:th * P + P],
                                                  ident[0:IDX_HEADS, 0:IDX_HEADS])
                    ins.then_inc(psum_filled, 1)
                elif what == "logits":
                    query_key(name, quad[g % 2], ik[:, :])
                elif what == "scores":
                    query_key(name, quad[g % 2], keys[:, g, :])
                elif what == "T":
                    set_free(name)
                    pe.wait_ge(probs_ready, probs_before[0] + X_HEADS + 2 * (g + 1))
                    for b in range(BANKS):
                        for n in range(KEYS // P):
                            ins = nc.tensor.transpose(banks(name)[:, b, n * P:n * P + P], probs[:, b, n * P:n * P + P], ident)
                    ins.then_inc(psum_filled, 1)
                else:
                    set_free(name)
                    read_out(pe, ("T", g))
                    if g == 0:
                        read_out(pe, "values")
                    for b in range(BANKS):
                        mm(banks(name)[:, b, 0:T], values[:, 0, g * P:g * P + P], probsT[:, b, 0:T], start=True, stop=False)
                        ins = mm(banks(name)[:, b, P:T], values[:, 1, g * P:g * P + P], probsT[:, b, T:KEYS], start=False, stop=True)
                    ins.then_inc(psum_filled, 1)

            for name in SPARSE:
                beside = {}
                for unit, turn in BESIDE.get(name, ()):
                    beside.setdefault(unit, []).append(turn)
                between = {unit: lambda turns=turns: [sparse_turn(turn) for turn in turns] for unit, turns in beside.items()}
                if name == "idx":
                    index_group()
                    continue
                if name == "values":
                    token_group(name, in_X, between)
                elif name[0] == "att_out":
                    def head_there(k):
                        if HEADS - BANKS <= k < HEADS - 1:
                            pe.wait_ge(last_heads, k - (HEADS - BANKS) + 1)
                        elif k % BANKS == 0 or k == HEADS - 1:
                            read_out(pe, ("o", k // BANKS))

                    named(name, in_attended, head_there, between=between)
                elif name == ("iq", 0):
                    named(name, in_X, next_x)
                    sum_squares("before_mix1")
                else:
                    named(name, in_X, between=between)
            for g in range(1, OUT_GROUPS):
                named(("att_out", g), in_attended, bank_by_bank=g == OUT_GROUPS - 1)
            sum_squares("mixed1")
            cross_attention(1)
            ffn(1)


def _units(w):
    k = w.shape[0] // (2 * P)
    return w.reshape(k, 2, P, BANKS * P).transpose(0, 2, 1, 3).reshape(k, P, UNIT)


def kernel(**inputs):
    import concourse.bacc as bacc
    from concourse.bass_utils import run_bass_kernel_spmd

    a = {k: np.asarray(v) for k, v in inputs.items()}
    w_in, w_out = a["dsa_w_in"][0], a["dsa_w_out"][0]
    edges = np.cumsum([0, HEADS * P, KV_HEADS * P, KV_HEADS * P, IDX_HEADS * P, P, IDX_HEADS])
    q, k, v, iq, ik, iw = (w_in[:, x:y] for x, y in zip(edges, edges[1:]))
    W = BANKS * P
    stream = np.empty((UNITS, P, UNIT), np.float32)
    plan = Plan()
    for name, n in plan.weights:
        at = plan.start[name]
        kind, l, g = (tuple(name) if isinstance(name, tuple) else (name,)) + (None,) * (3 - (len(name) if isinstance(name, tuple) else 1))
        cols = lambda w, g: w[:, g * W:(g + 1) * W]
        if kind == "idx":
            both = np.concatenate([ik, iw, np.zeros((D, 2 * P - P - IDX_HEADS), np.float32)], 1)
            stream[at:at + n] = both.reshape(n, 4, P, 2 * P).transpose(0, 2, 1, 3).reshape(n, P, UNIT)
            continue
        if kind == "mem_keys":
            w = cols(a["xattn_wkv"][l], 0)
        elif kind == "mem_values":
            w = cols(a["xattn_wkv"][l], 1)
        elif kind == "pool":
            w = a["pool_w"][0, l]
        elif kind == "cross_q":
            w = a["xattn_wq"][l]
        elif kind == "cross_out":
            w = cols(a["xattn_wo"][l], g)
        elif kind == "glu":
            gate = a["ffn_w_gate_up"][l][:, 2 * P * g:2 * P * (g + 1)]
            up = a["ffn_w_gate_up"][l][:, D_FF + 2 * P * g:D_FF + 2 * P * (g + 1)]
            w = np.concatenate([gate, up], 1)
        elif kind == "down":
            w = cols(a["ffn_w_down"][l], g)
        elif kind == "iq":
            w = cols(iq, l)
        elif kind == "q":
            w = cols(q, l)
        elif kind == "keys":
            w = k
        elif kind == "values":
            w = v
        else:
            w = cols(w_out, l)
        stream[at:at + n] = _units(w)

    def by_feature(x):
        return np.ascontiguousarray(x.T.reshape(C, P, x.shape[0]).transpose(1, 0, 2))

    gains = np.concatenate([a["norm_gains"].reshape(6 * LAYERS, D), a["mem_norm"][None], a["pool_scale"]])
    vectors = np.ascontiguousarray(gains.reshape(N_GAINS, C, P).transpose(2, 0, 1))
    consts = np.zeros((P, N_CONST), np.float32)
    put = lambda name, x: consts.__setitem__((slice(0, x.shape[0]), slice(CONST_AT[name], CONST_AT[name] + CONST[name])), x)
    put("ident", np.eye(P, dtype=np.float32))
    put("ones", np.ones((P, P), np.float32))
    query, key = np.arange(P)[:, None], np.arange(T)[None]
    put("causal", np.concatenate([np.where(key[:, :P] <= query, 0, NEG), np.where(key <= query + P, 0, NEG)], 1).astype(np.float32))
    t_in, t_out = np.arange(P)[:, None], np.arange(T)[None]
    averages = np.zeros((P, len(POOL_WINDOWS), REACH + P), np.float32)
    for n, w in enumerate(POOL_WINDOWS):
        for t_from, cols, at in ((0, slice(0, REACH), slice(0, REACH)), (P, slice(P, T), slice(REACH, REACH + P))):
            age = t_out - (t_in + t_from)
            mean = ((age >= 0) & (age < w)) / np.minimum(t_out + 1, w).astype(np.float32) - (age == 0)
            averages[:, n, at] = mean[:, cols]
    inv = np.float32(500000.0) ** (-np.arange(0, ROT, 2, dtype=np.float32) / np.float32(ROT))
    put("inv", np.concatenate([inv, inv])[:, None])
    put("sign", np.concatenate([-np.ones(ROT // 2), np.ones(ROT // 2)])[:, None].astype(np.float32))
    put("eps", np.full((P, 1), EPS, np.float32))
    arrays = {
        "xT": by_feature(a["x"][0]), "x_tokens": np.ascontiguousarray(a["x"][0].reshape(HALVES, P, D).transpose(1, 0, 2)),
        "memT": by_feature(a["mem"][0]), "positions": np.ascontiguousarray(a["positions"], np.int32), "averages": averages,
        "vectors": vectors, "constants": consts, "weights": stream,
    }
    nc = bacc.Bacc("TRN2", target_bir_lowering=False, num_devices=1)
    args = [nc.dram_tensor(n, x.shape, mybir.dt.from_np(x.dtype), kind="ExternalInput").ap() for n, x in arrays.items()]
    out = nc.dram_tensor("outT", (P, C, T), F32, kind="ExternalOutput").ap()
    kv_store = nc.dram_tensor("kv_store", (P, 2, BANKS, T), F32, kind="Internal").ap()
    hybrid_trunk(nc, *args, out, kv_store)
    result = run_bass_kernel_spmd(nc, [arrays], core_ids=[0])
    got = result.results[0]["outT"]
    return np.ascontiguousarray(got.transpose(2, 1, 0).reshape(1, T, D))
```
